# Optimizing a Trainium2 kernel written in Bass

```python
import jax, jax.numpy as jnp
from jax import lax
import numpy as np

D_MODEL = 1024
BATCH = 1
SEQ = 512
DEPTH = 2

HEAD_DIM = 64
FOX_HEADS = 16
SWA_Q_HEADS = 16
SWA_KV_HEADS = 2
SWA_GROUP = SWA_Q_HEADS // SWA_KV_HEADS
WINDOW = 128
BLOCK = 128
D_FF = 4 * D_MODEL
ROPE_THETA = 10000.0
NORM_EPS = 1e-6
N_MIXERS = 2
N_FOX = (DEPTH + 1) // 2
N_SWA = DEPTH // 2
FOX_IN = 3 * FOX_HEADS * HEAD_DIM + FOX_HEADS
SWA_IN = (SWA_Q_HEADS + 2 * SWA_KV_HEADS) * HEAD_DIM

kernel_name = "fox_swa_sink_hybrid_sandwich"

def rms_norm(x, g):
    xf = x.astype(jnp.float32)
    y = xf * lax.rsqrt(jnp.mean(xf * xf, axis=-1, keepdims=True) + NORM_EPS)
    return (y * g.astype(jnp.float32)).astype(x.dtype)

def rope(x, positions):
    half = HEAD_DIM // 2
    inv_freq = 1.0 / (ROPE_THETA ** (jnp.arange(0, HEAD_DIM, 2, dtype=jnp.float32) / HEAD_DIM))
    ang = positions.astype(jnp.float32)[..., None] * inv_freq
    cos = jnp.cos(ang)[:, :, None, :].astype(x.dtype)
    sin = jnp.sin(ang)[:, :, None, :].astype(x.dtype)
    x1, x2 = x[..., :half], x[..., half:]
    return jnp.concatenate([x1 * cos - x2 * sin, x2 * cos + x1 * sin], axis=-1)

def fox_attention(h, w_in, b_f, w_out):
    B, S, _ = h.shape
    nb = S // BLOCK
    hd_all = FOX_HEADS * HEAD_DIM
    proj = h @ w_in
    scale = HEAD_DIM ** -0.5
    q = proj[..., :hd_all].reshape(B, S, FOX_HEADS, HEAD_DIM) * scale
    k = proj[..., hd_all:2 * hd_all].reshape(B, S, FOX_HEADS, HEAD_DIM)
    v = proj[..., 2 * hd_all:3 * hd_all].reshape(B, S, FOX_HEADS, HEAD_DIM)
    log_f = jax.nn.log_sigmoid((proj[..., 3 * hd_all:] + b_f).astype(jnp.float32))
    c = jnp.cumsum(log_f, axis=1).transpose(0, 2, 1)
    qb = q.transpose(0, 2, 1, 3).reshape(B, FOX_HEADS, nb, BLOCK, HEAD_DIM).transpose(2, 0, 1, 3, 4)
    cq = c.reshape(B, FOX_HEADS, nb, BLOCK).transpose(2, 0, 1, 3)
    kt = k.transpose(0, 2, 1, 3)
    vt = v.transpose(0, 2, 1, 3)
    key_pos = jnp.arange(S)

    def query_block(args):
        q_blk, c_blk, i = args
        s = jnp.einsum('bhqd,bhkd->bhqk', q_blk, kt, preferred_element_type=jnp.float32)
        s = s + c_blk[..., None] - c[:, :, None, :]
        q_pos = i * BLOCK + jnp.arange(BLOCK)
        s = jnp.where(key_pos[None, :] <= q_pos[:, None], s, -jnp.inf)
        p = jax.nn.softmax(s, axis=-1).astype(vt.dtype)
        return jnp.einsum('bhqk,bhkd->bhqd', p, vt)

    o = lax.map(query_block, (qb, cq, jnp.arange(nb)))
    o = o.transpose(1, 0, 3, 2, 4).reshape(B, S, hd_all)
    return o @ w_out

def swa_sink_attention(h, positions, w_in, sinks, w_out):
    B, S, _ = h.shape
    nb = S // BLOCK
    qd = SWA_Q_HEADS * HEAD_DIM
    kvd = SWA_KV_HEADS * HEAD_DIM
    proj = h @ w_in
    scale = HEAD_DIM ** -0.5
    q = rope(proj[..., :qd].reshape(B, S, SWA_Q_HEADS, HEAD_DIM), positions) * scale
    k = rope(proj[..., qd:qd + kvd].reshape(B, S, SWA_KV_HEADS, HEAD_DIM), positions)
    v = proj[..., qd + kvd:].reshape(B, S, SWA_KV_HEADS, HEAD_DIM)
    q = q.reshape(B, nb, BLOCK, SWA_KV_HEADS, SWA_GROUP, HEAD_DIM)
    k = k.reshape(B, nb, BLOCK, SWA_KV_HEADS, HEAD_DIM)
    v = v.reshape(B, nb, BLOCK, SWA_KV_HEADS, HEAD_DIM)

    def band(t):
        prev = jnp.pad(t, ((0, 0), (1, 0), (0, 0), (0, 0), (0, 0)))[:, :-1]
        return jnp.concatenate([prev, t], axis=2)

    kb, vb = band(k), band(v)
    s = jnp.einsum('bnqhgd,bnshd->bhgnqs', q, kb, preferred_element_type=jnp.float32)
    qi = jnp.arange(BLOCK)[:, None]
    kj = jnp.arange(2 * BLOCK)[None, :]
    diff = qi + BLOCK - kj
    in_window = (diff >= 0) & (diff < WINDOW)
    key_exists = (jnp.arange(nb)[:, None, None] > 0) | (kj >= BLOCK)[None]
    mask = in_window[None] & key_exists
    s = jnp.where(mask, s, -jnp.inf)
    sink = sinks.astype(jnp.float32).reshape(SWA_KV_HEADS, SWA_GROUP)[None, :, :, None, None, None]
    m = jnp.maximum(jnp.max(s, axis=-1, keepdims=True), sink)
    e = jnp.exp(s - m)
    denom = jnp.sum(e, axis=-1, keepdims=True) + jnp.exp(sink - m)
    p = (e / denom).astype(vb.dtype)
    o = jnp.einsum('bhgnqs,bnshd->bnqhgd', p, vb).reshape(B, S, qd)
    return o @ w_out

def squared_relu_mlp(h, w_up, w_down):
    return jnp.square(jax.nn.relu(h @ w_up)) @ w_down

def setup_inputs(seed: int = 0) -> dict:
    key = jax.random.key(seed)
    ks = jax.random.split(key, 14)
    f32 = jnp.float32
    nrm = lambda k, shape, s: jax.random.normal(k, shape, f32) * s
    return {
        "x": nrm(ks[0], (BATCH, SEQ, D_MODEL), 1.0),
        "positions": jnp.broadcast_to(jnp.arange(SEQ, dtype=jnp.int32)[None, :], (BATCH, SEQ)),
        "fox_w_in": nrm(ks[1], (N_FOX, D_MODEL, FOX_IN), D_MODEL ** -0.5),
        "fox_b_f": 3.0 + nrm(ks[2], (N_FOX, FOX_HEADS), 1.0),
        "fox_w_out": nrm(ks[3], (N_FOX, FOX_HEADS * HEAD_DIM, D_MODEL), (FOX_HEADS * HEAD_DIM) ** -0.5),
        "swa_w_in": nrm(ks[4], (N_SWA, D_MODEL, SWA_IN), D_MODEL ** -0.5),
        "swa_sinks": nrm(ks[5], (N_SWA, SWA_Q_HEADS), 0.5),
        "swa_w_out": nrm(ks[6], (N_SWA, SWA_Q_HEADS * HEAD_DIM, D_MODEL), (SWA_Q_HEADS * HEAD_DIM) ** -0.5),
        "norm_pre_mix": 1.0 + nrm(ks[7], (DEPTH, D_MODEL), 0.02),
        "norm_post_mix": 1.0 + nrm(ks[8], (DEPTH, D_MODEL), 0.02),
        "norm_pre_ffn": 1.0 + nrm(ks[9], (DEPTH, D_MODEL), 0.02),
        "norm_post_ffn": 1.0 + nrm(ks[10], (DEPTH, D_MODEL), 0.02),
        "mlp_w_up": nrm(ks[11], (DEPTH, D_MODEL, D_FF), D_MODEL ** -0.5),
        "mlp_w_down": nrm(ks[12], (DEPTH, D_FF, D_MODEL), D_FF ** -0.5),
    }

def reference(x, positions, fox_w_in, fox_b_f, fox_w_out, swa_w_in, swa_sinks, swa_w_out,
              norm_pre_mix, norm_post_mix, norm_pre_ffn, norm_post_ffn, mlp_w_up, mlp_w_down):
    for i in range(DEPTH):
        j = i // N_MIXERS
        h = rms_norm(x, norm_pre_mix[i])
        if i % N_MIXERS == 0:
            h = fox_attention(h, fox_w_in[j], fox_b_f[j], fox_w_out[j])
        else:
            h = swa_sink_attention(h, positions, swa_w_in[j], swa_sinks[j], swa_w_out[j])
        x = x + rms_norm(h, norm_post_mix[i])
        h = rms_norm(x, norm_pre_ffn[i])
        h = squared_relu_mlp(h, mlp_w_up[i], mlp_w_down[i])
        x = x + rms_norm(h, norm_post_ffn[i])
    return x


_drawn_inputs = setup_inputs


def setup_inputs(seed=0):
    import zlib

    import numpy as np

    out = dict(_drawn_inputs(seed))
    spreads = {}
    factors = {'swa_sinks': 7.165, 'norm_post_mix': 3.006, 'norm_pre_ffn': 3.299, 'norm_post_ffn': 10.1}
    for name, (base, spread) in spreads.items():
        noise = np.random.default_rng([zlib.crc32(name.encode()), seed]).standard_normal(out[name].shape)
        drawn = base * np.exp(spread * noise) if base else spread * noise
        out[name] = __import__('jax').numpy.asarray(drawn.astype(out[name].dtype))
    for name, factor in factors.items():
        out[name] = (out[name] * factor).astype(out[name].dtype)
    return out
```

```python
from contextlib import ExitStack

import numpy as np

import concourse.bass as bass
from concourse import mybir

F32 = mybir.dt.float32
F32R = mybir.dt.float32r
I32 = mybir.dt.int32
ALU = mybir.AluOpType
ACT = mybir.ActivationFunctionType
AX_X = mybir.AxisListType.X

P = 128
SEQ = 512
D = 1024
D_FF = 4096
HD = 64
HEADS = 16
KV_HEADS = 2
GROUP = HEADS // KV_HEADS
NB = SEQ // P
KT = D // P
PAIRS = HEADS // 2
QD = HEADS * HD
KVD = KV_HEADS * HD
FOX_IN = 3 * QD + HEADS
EPS = 1e-6
SCALE = HD ** -0.5
NEG = -1e30
ROPE_THETA = 10000.0

RING = 4
RAW = 2
AHEAD = RING - 1

F_CHUNK = 16
CHUNKS = D_FF // P // F_CHUNK
HALVES = F_CHUNK // KT

W_FOX = 0
W_FOX_OUT = W_FOX + 1 + 3 * PAIRS
W_MLP = [W_FOX_OUT + KT, 0]
MLP_TILES = CHUNKS * (F_CHUNK + KT * HALVES)
W_SWA = W_MLP[0] + MLP_TILES
W_SWA_OUT = W_SWA + 2 + PAIRS
W_MLP[1] = W_SWA_OUT + KT
W_END = W_MLP[1] + MLP_TILES
G_FOX = 0
G_FOX_OUT = G_FOX + 1 + 3 * PAIRS
G_MLP = [G_FOX_OUT + KT, 0]
MLP_GROUPS = CHUNKS * (F_CHUNK + KT)
G_SWA = G_MLP[0] + MLP_GROUPS
G_SWA_OUT = G_SWA + 2 + PAIRS
G_MLP[1] = G_SWA_OUT + KT

FOX_OFF = [0, 128, 384, 768]
FOX_PT = [0, 512, 896, 1152]
FOX_P = 1280
SWA_P = NB * 2 * P


def inv_freq():
    return np.float32(1) / (ROPE_THETA ** (np.arange(0, HD, 2) / HD)).astype(np.float32)


def two_pi_parts():
    rest, parts = 2 * np.pi, []
    for _ in range(5):
        step = 2.0 ** (np.floor(np.log2(rest)) - 5)
        parts.append(float(np.floor(rest / step) * step))
        rest -= parts[-1]
    return parts + [float(np.float32(rest))]


def trunk(nc, x, positions, fox_w_in, fox_b_f, fox_w_out, swa_w_in, swa_sinks, swa_w_out,
          norm_pre_mix, norm_post_mix, norm_pre_ffn, norm_post_ffn, mlp_w_up, mlp_w_down, out):
    with ExitStack() as ctx:
        def sb(name, shape, dt=F32):
            return ctx.enter_context(nc.sbuf_tensor(name, shape, dt))

        def sem(name):
            return ctx.enter_context(nc.semaphore(name))

        xT = sb("xT", [P, KT, SEQ])
        yT = sb("yT", [P, KT, SEQ])
        h_hi = sb("h_hi", [P, KT, SEQ], F32R)
        h_lo = sb("h_lo", [P, KT, SEQ], F32R)
        w_raw = sb("w_raw", [P, RAW, KT, P])
        w_hi = sb("w_hi", [P, RING, KT, P], F32R)
        w_lo = sb("w_lo", [P, RING, KT, P], F32R)
        act = sb("act", [P, 32, SEQ], F32R)
        pt_hi = sb("pt_hi", [P, FOX_P], F32R)
        pt_lo = sb("pt_lo", [P, FOX_P], F32R)
        v_hi = sb("v_hi", [P, 2, NB, P], F32R)
        v_lo = sb("v_lo", [P, 2, NB, P], F32R)
        tmp = sb("tmp", [P, 4, SEQ])
        rstd = sb("rstd", [P, SEQ])
        cos_t = sb("cos_t", [P, SEQ])
        sin_t = sb("sin_t", [P, SEQ])
        ident = sb("ident", [P, P])
        ones = sb("ones", [P, P])
        ident_r = sb("ident_r", [P, P], F32R)
        masks = sb("masks", [P, 2, 4 * P], F32R)
        gains = sb("gains", [P, 4, 2, KT])
        freq_row = sb("freq_row", [1, P])
        freq = sb("freq", [P, 1])
        sign = sb("sign", [P, 1])
        b_f = sb("b_f", [P, 1])
        sinks = sb("sinks", [P, HEADS])
        nsinks = sb("nsinks", [P, HEADS])
        pool_flag = sb("pool_flag", [P, 1])
        nmax = sb("nmax", [P, 2, NB])
        rsum = sb("rsum", [P, 2, NB])
        esink = sb("esink", [P, 2, NB])
        rden = sb("rden", [P, 2, NB])

        o_hi, o_lo = act[:, 0:8, :], act[:, 8:16, :]
        u_hi, u_lo = act[:, 0:F_CHUNK, :], act[:, F_CHUNK:2 * F_CHUNK, :]
        y_flat = yT[:, :, :].rearrange("p k t -> p (k t)")
        prob = [y_flat[:, h * FOX_P:(h + 1) * FOX_P] for h in range(2)]
        rope = [y_flat[:, (5 + i) * SEQ:(6 + i) * SEQ] for i in range(3)]
        x_in = y_flat.rearrange("p (b d) -> p b d", b=NB)
        mask_src = xT[:, KT - 2:KT, :]

        def fox_ops(p, side):
            s = 16 + 8 * (p % 2) + 4 * side
            return act[:, s, :], act[:, s + 1, :], act[:, s + 2, :], act[:, s + 3, :]

        def swa_q(p, side):
            s = 16 + 4 * (p % 2) + 2 * side
            return act[:, s, :], act[:, s + 1, :]

        def swa_k(kv, side):
            return act[:, 24 + kv, :], act[:, 26 + 2 * kv + side, :]

        def half(side):
            return slice(HD * side, HD * side + HD)

        def bank(name):
            return ctx.enter_context(nc.psum_tensor(name, [P, SEQ], F32))

        acc = [bank(f"acc{i}") for i in range(2)]
        logit = [bank(f"logit{i}") for i in range(2)]
        trans = [bank(f"trans{i}") for i in range(2)]
        mix = [bank(f"mix{i}") for i in range(2)]

        c_dram = nc.dram_tensor("c_scratch", (HEADS, 2, SEQ), F32R).ap()

        raw_landed = [sem(f"raw_landed{i}") for i in range(RAW)]
        whi_done = sem("whi_done")
        wlo_done = sem("wlo_done")
        used = sem("used")
        acc_free = sem("acc_free")
        x_landed = sem("x_landed")
        small_landed = sem("small_landed")
        pos_landed = sem("pos_landed")
        pool_step = sem("pool_step")
        const_done = sem("const_done")
        mask_done = sem("mask_done")
        freq_t = sem("freq_t")
        freq_done = sem("freq_done")
        angle_done = sem("angle_done")
        table_done = sem("table_done")
        xt_ready = sem("xt_ready")
        x_done = sem("x_done")
        sq_done = sem("sq_done")
        stat_done = sem("stat_done")
        ms_done = sem("ms_done")
        r0_step = sem("r0_step")
        hf_done = sem("hf_done")
        hh_done = sem("hh_done")
        h_done = sem("h_done")
        dve_step = sem("dve_step")
        relu_done = sem("relu_done")
        uhi_done = sem("uhi_done")
        u_done = sem("u_done")
        gate_step = sem("gate_step")
        gate_act = sem("gate_act")
        c_done = sem("c_done")
        c_stored = sem("c_stored")
        aug_set = sem("aug_set")
        aug_landed = [sem(f"aug_landed{i}") for i in range(2)]
        q_done = sem("q_done")
        hi_done = sem("hi_done")
        vh_done = sem("vh_done")
        s_ready = sem("s_ready")
        max_done = sem("max_done")
        exp_done = sem("exp_done")
        prob_done = sem("prob_done")
        t_ready = sem("t_ready")
        th_done = sem("th_done")
        t_free = sem("t_free")
        pv_done = sem("pv_done")
        oh_done = sem("oh_done")
        o_done = sem("o_done")
        rot_done = sem("rot_done")
        rope_done = sem("rope_done")
        es_done = sem("es_done")
        fin_ready = sem("fin_ready")
        fin_done = sem("fin_done")
        stored = sem("stored")

        block = ctx.enter_context(nc.Block())

        def fox_t(hd, i):
            return 7 * (hd // 2) + 1 + 3 * (hd % 2) + i

        FOX_S, FOX_T = HEADS * NB, PAIRS * 7
        SWA_T0 = FOX_T + 1

        @block.sync
        def _(sp):
            xr = x.rearrange("a (b p) d -> p (a b) d", p=P)
            for b in range(NB):
                sp.dma_start(x_in[:, b, :], xr[:, b, :]).then_inc(x_landed, 16)

            def load(n, src):
                if n >= RAW:
                    sp.wait_ge(wlo_done, n - RAW + 1)
                sp.dma_start(w_raw[:, n % RAW, :, :],
                             src.rearrange("(k p) n -> p k n", p=P)).then_inc(raw_landed[n % RAW], 16)

            w_in = fox_w_in[0]
            load(W_FOX, w_in[:, FOX_IN - P:FOX_IN])
            for p in range(PAIRS):
                for j in range(3):
                    load(W_FOX + 1 + 3 * p + j, w_in[:, j * QD + p * P:j * QD + (p + 1) * P])
            for o in range(KT):
                load(W_FOX_OUT + o, fox_w_out[0][:, o * P:(o + 1) * P])

            def load_mlp(layer):
                n = W_MLP[layer]
                for c in range(CHUNKS):
                    for j in range(F_CHUNK):
                        f = (c * F_CHUNK + j) * P
                        load(n, mlp_w_up[layer][:, f:f + P])
                        n += 1
                    for o in range(KT):
                        for hf in range(HALVES):
                            f = (c * F_CHUNK + hf * KT) * P
                            load(n, mlp_w_down[layer][f:f + KT * P, o * P:(o + 1) * P])
                            n += 1

            load_mlp(0)
            w_in2 = swa_w_in[0]
            load(W_SWA, w_in2[:, QD:QD + KVD])
            load(W_SWA + 1, w_in2[:, QD + KVD:QD + 2 * KVD])
            for p in range(PAIRS):
                load(W_SWA + 2 + p, w_in2[:, p * P:(p + 1) * P])
            for o in range(KT):
                load(W_SWA_OUT + o, swa_w_out[0][:, o * P:(o + 1) * P])
            load_mlp(1)

            outr = out.rearrange("a (b p) (k f) -> k p (a b) f", p=P, f=P)
            for k in range(KT):
                sp.wait_ge(fin_done, k + 1)
                sp.dma_start(outr[k], yT[:, k, :].rearrange("p (b f) -> p b f", b=NB)).then_inc(stored, 16)
            sp.wait_ge(stored, 16 * KT)

        @block.gpsimd
        def _(pool):
            step = [0]

            def done(ins):
                step[0] += 1
                ins.then_inc(pool_step, 1)
                pool.wait_ge(pool_step, step[0])

            pos_i = tmp[:, 3, :].bitcast(I32)
            pool.dma_start(pos_i, positions.broadcast_to([P, SEQ])).then_inc(pos_landed, 16)
            done(nc.gpsimd.memset(b_f[:, :], 0.0))
            with nc.allow_non_contiguous_dma(reason="small vectors, feature-major"):
                for i, g in enumerate((norm_pre_mix, norm_post_mix, norm_pre_ffn, norm_post_ffn)):
                    for layer in range(2):
                        pool.dma_start(gains[:, i, layer, :],
                                       g[layer].rearrange("(k p) -> p k", p=P)).then_inc(small_landed, 16)
                pool.dma_start(b_f[P - HEADS:P, :], fox_b_f.rearrange("a h -> h a")).then_inc(small_landed, 16)
            pool.dma_start(sinks[:, :], swa_sinks.broadcast_to([P, HEADS])).then_inc(small_landed, 16)

            for i, f in enumerate(inv_freq()):
                for q in range(4):
                    last = nc.gpsimd.memset(freq_row[0:1, q * 32 + i:q * 32 + i + 1], float(f))
            done(last)
            done(nc.gpsimd.memset(sign[:, :], 1.0))
            done(nc.gpsimd.memset(ones[:, :], 1.0))
            done(nc.gpsimd.memset(ident[:, :], 0.0))
            done(nc.gpsimd.memset(sign[0:32, :], -1.0))
            done(nc.gpsimd.memset(sign[64:96, :], -1.0))
            done(nc.gpsimd.affine_select(out=ident[:, :], in_=ident[:, :], compare_op=ALU.not_equal, fill=1.0,
                                         base=0, pattern=[[-1, P]], channel_multiplier=1))
            done(nc.gpsimd.memset(mask_src, 0.0))
            done(nc.gpsimd.memset(mask_src[:, 0, 0:P], NEG))
            for a, at, causal in ((0, 1, 1), (0, 2, 0), (0, 3, 1), (1, 0, 0), (1, 1, 1), (1, 2, 0), (1, 3, 1)):
                m = mask_src[:, a, at * P:(at + 1) * P]
                sgn = 1 if causal else -1
                done(nc.gpsimd.affine_select(out=m, in_=m, compare_op=ALU.is_ge if causal else ALU.is_gt, fill=NEG,
                                             base=0, pattern=[[-sgn, P]], channel_multiplier=sgn))
            nc.gpsimd.memset(pool_flag[:, :], 0.0).then_inc(const_done, 1)
            pool.wait_ge(const_done, 1)

            for p in range(2):
                for side in range(2):
                    _, q2, _, k2 = fox_ops(p, side)
                    o = HD * (1 - side)
                    done(nc.gpsimd.memset(q2[half(1 - side), :].bitcast(F32), 0.0))
                    done(nc.gpsimd.memset(k2[half(1 - side), :].bitcast(F32), 0.0))
                    done(nc.gpsimd.memset(q2[o:o + 4, :].bitcast(F32), -1.0))
                    done(nc.gpsimd.memset(k2[o:o + 4, :].bitcast(F32), 1.0))
            pool.wait_ge(c_done, 1)
            pool.dma_start(c_dram[:, 0, :], pt_hi[P - HEADS:P, 0:SEQ]).then_inc(c_stored, 16)
            pool.dma_start(c_dram[:, 1, :], pt_lo[P - HEADS:P, 0:SEQ]).then_inc(c_stored, 16)
            pool.wait_ge(c_stored, 32)
            for p in range(PAIRS):
                if p >= 2:
                    pool.wait_ge(s_ready, 2 * NB * (p - 1))
                for side in range(2):
                    _, q2, _, k2 = fox_ops(p, side)
                    o = HD * (1 - side)
                    pool.dma_start(q2[o:o + 2, :], c_dram[2 * p + side]).then_inc(aug_landed[p % 2], 16)
                    pool.dma_start(k2[o + 2:o + 4, :], c_dram[2 * p + side]).then_inc(aug_landed[p % 2], 16)

            pool.wait_ge(used, W_SWA)
            for p in range(2):
                for side in range(2):
                    done(nc.gpsimd.memset(swa_q(p, side)[1][half(1 - side), :].bitcast(F32), 0.0))
                    done(nc.gpsimd.memset(swa_k(p, side)[1][half(1 - side), :].bitcast(F32), 0.0))
            nc.gpsimd.memset(pool_flag[:, :], 0.0).then_inc(aug_set, 1)

        @block.tensor
        def _(pe):
            def project(n, g, rhs_hi, rhs_lo, k0=0, k1=KT, first=True, last=True, rhs_ready=None):
                if k0 == 0:
                    pe.wait_ge(wlo_done, n + 1)
                    if first and g >= 2:
                        pe.wait_ge(acc_free, g - 1)
                s, a = n % RING, acc[g % 2]
                for k in range(k0, k1):
                    if rhs_ready:
                        rhs_ready(k)
                    nc.tensor.matmul(a[:, :], w_hi[:, s, k, :], rhs_hi(k), start=first and k == 0, stop=False)
                    nc.tensor.matmul(a[:, :], w_hi[:, s, k, :], rhs_lo(k), start=False, stop=False)
                    mm = nc.tensor.matmul(a[:, :], w_lo[:, s, k, :], rhs_hi(k), start=False,
                                          stop=last and k == KT - 1)
                return mm

            def finish(mm):
                mm.then_inc(used, 1)

            def of(t):
                return lambda k: t[:, k, :]

            def stat(norm, k):
                pe.wait_ge(sq_done, norm * KT + k + 1)
                nc.tensor.matmul(mix[norm % 2][:, :], ones[:, :], tmp[:, k % 2, :], start=(k == 0),
                                 stop=(k == KT - 1)).then_inc(stat_done, 1)

            pe.wait_ge(const_done, 1)
            nc.tensor.transpose(mix[1][:, 0:1], freq_row[0:1, :], ident[0:1, 0:1]).then_inc(freq_t, 1)
            pe.wait_ge(x_landed, 16 * NB)
            for k in range(KT):
                if k >= 2:
                    pe.wait_ge(x_done, k - 1)
                for b in range(NB):
                    mm = nc.tensor.transpose(trans[k % 2][:, b * P:(b + 1) * P], x_in[:, b, k * P:(k + 1) * P],
                                             ident[:, :])
                mm.then_inc(xt_ready, 1)
                if k >= 1:
                    stat(0, k - 1)
            stat(0, KT - 1)

            def h_ready(norm):
                return lambda k: pe.wait_ge(h_done, norm * KT + k + 1)

            finish(project(W_FOX, G_FOX, of(h_hi), of(h_lo), rhs_ready=h_ready(0)))

            def fox_proj(pair, k0, k1):
                if pair == PAIRS:
                    return
                while k0 < k1:
                    j, a = divmod(k0, KT)
                    b = min(KT, a + k1 - k0)
                    mm = project(W_FOX + 1 + 3 * pair + j, G_FOX + 1 + 3 * pair + j, of(h_hi), of(h_lo), a, b)
                    if b == KT:
                        finish(mm)
                    k0 += b - a

            def fox_logits(hd, qb):
                p, side = divmod(hd, 2)
                j = hd * NB + qb
                if side == 0 and qb == 0:
                    pe.wait_ge(acc_free, G_FOX + 3 * p + 3)
                    pe.wait_ge(aug_landed[p % 2], 64 * (p // 2 + 1))
                if j == 0:
                    pe.wait_ge(mask_done, 1)
                if j >= 2:
                    pe.wait_ge(exp_done, j - 1)
                q1, q2, k1, k2 = fox_ops(p, side)
                n, qs = (qb + 1) * P, slice(qb * P, (qb + 1) * P)
                s = logit[j % 2]
                nc.tensor.matmul(s[:, 0:n], q1[:, qs], k1[:, 0:n], start=True, stop=False)
                nc.tensor.matmul(s[:, 0:n], q2[:, qs], k2[:, 0:n], start=False, stop=False)
                nc.tensor.matmul(s[:, qs], ident_r[:, :], masks[:, 0, P:2 * P], start=False,
                                 stop=True).then_inc(s_ready, 1)

            def fox_transposes(hd, i):
                j = fox_t(hd, i)
                if i == 0:
                    pe.wait_ge(prob_done, hd + 1)
                pe.wait_ge(t_free, j - 1) if j >= 2 else None
                at = 0
                for kb in ((0,), (1,), (2, 3))[i]:
                    for qb in range(kb, NB):
                        c = FOX_OFF[qb] + kb * P
                        mm = nc.tensor.transpose(trans[j % 2][:, at:at + P], prob[hd % 2][:, c:c + P], ident[:, :])
                        at += P
                mm.then_inc(t_ready, 1)

            def value_transposes(j, g):
                pe.wait_ge(acc_free, g + 1)
                if j >= 2:
                    pe.wait_ge(t_free, j - 1)
                for b in range(NB):
                    mm = nc.tensor.transpose(trans[j % 2][:, b * P:(b + 1) * P], tmp[:, 0, b * P:(b + 1) * P],
                                             ident[:, :])
                mm.then_inc(t_ready, 1)

            def fox_mix(hd):
                p = hd // 2
                pe.wait_ge(t_free, fox_t(hd, 2) + 1)
                if hd >= 2:
                    pe.wait_ge(o_done, hd - 1)
                o = mix[hd % 2]
                for kb in range(NB):
                    n = (NB - kb) * P
                    pt = slice(FOX_PT[kb], FOX_PT[kb] + n)
                    for v, t in ((v_hi, pt_hi), (v_hi, pt_lo), (v_lo, pt_hi)):
                        mm = nc.tensor.matmul(o[:, kb * P:SEQ], v[:, p % 2, kb, :], t[:, pt],
                                              start=(kb == 0 and v is v_hi and t is pt_hi),
                                              stop=(kb == NB - 1 and v is v_lo))
                mm.then_inc(pv_done, 1)

            fox_proj(0, 0, 3 * KT)
            for p in range(PAIRS):
                a, b, nxt = 2 * p, 2 * p + 1, p + 1
                fox_logits(a, 0)
                fox_logits(a, 1)
                fox_proj(nxt, 0, 2)
                value_transposes(7 * p, G_FOX + 3 + 3 * p)
                fox_logits(a, 2)
                fox_proj(nxt, 2, 4)
                fox_logits(a, 3)
                fox_proj(nxt, 4, 6)
                fox_logits(b, 0)
                fox_proj(nxt, 6, 8)
                fox_logits(b, 1)
                fox_proj(nxt, 8, 10)
                fox_transposes(a, 0)
                fox_transposes(a, 1)
                fox_logits(b, 2)
                fox_proj(nxt, 10, 12)
                fox_transposes(a, 2)
                fox_logits(b, 3)
                fox_proj(nxt, 12, 16)
                fox_mix(a)
                fox_proj(nxt, 16, 20)
                fox_transposes(b, 0)
                fox_transposes(b, 1)
                fox_proj(nxt, 20, 22)
                fox_transposes(b, 2)
                fox_proj(nxt, 22, 24)
                fox_mix(b)

            def out_proj(w0, g0, norm, heads0):
                for o in range(KT):
                    finish(project(w0 + o, g0 + o, of(o_hi), of(o_lo), rhs_ready=(
                        lambda k: pe.wait_ge(o_done, heads0 + 2 * k + 2)) if o == 0 else None))
                    if o >= 1:
                        stat(norm, o - 1)
                stat(norm, KT - 1)
                for k in range(KT):
                    stat(norm + 1, k)

            def mlp(layer, norm):
                n, g = W_MLP[layer], G_MLP[layer]
                for c in range(CHUNKS):
                    for j in range(F_CHUNK):
                        finish(project(n, g, of(h_hi), of(h_lo), rhs_ready=h_ready(norm // 2) if c == j == 0 else None))
                        n, g = n + 1, g + 1
                    done = (layer * CHUNKS + c) * F_CHUNK
                    for o in range(KT):
                        for hf in range(HALVES):
                            def u(t):
                                return lambda k: t[:, hf * KT + k, :]

                            def u_ready(k):
                                pe.wait_ge(u_done, done + hf * KT + k + 1)
                            finish(project(n, g, u(u_hi), u(u_lo), first=hf == 0, last=hf == HALVES - 1,
                                           rhs_ready=u_ready if o == 0 else None))
                            n += 1
                        g += 1
                        if c == CHUNKS - 1 and o >= 1:
                            stat(norm + 1, o - 1)
                stat(norm + 1, KT - 1)

            out_proj(W_FOX_OUT, G_FOX_OUT, 1, 0)
            mlp(0, 2)
            for k in range(KT):
                stat(4, k)

            finish(project(W_SWA, G_SWA, of(h_hi), of(h_lo), rhs_ready=h_ready(2)))
            finish(project(W_SWA + 1, G_SWA + 1, of(h_hi), of(h_lo)))

            def swa_proj(pair, k0, k1):
                if pair == PAIRS:
                    return
                mm = project(W_SWA + 2 + pair, G_SWA + 2 + pair, of(h_hi), of(h_lo), k0, k1)
                if k1 == KT:
                    finish(mm)

            def swa_logits(hd, i):
                p, side = divmod(hd, 2)
                j = FOX_S + hd * 2 + i
                if side == 0 and i == 0:
                    pe.wait_ge(q_done, p + 2)
                    if p == 0:
                        pe.wait_ge(aug_set, 1)
                pe.wait_ge(exp_done, j - 1)
                q1, q2 = swa_q(p, side)
                k1, k2 = swa_k(hd // GROUP, side)
                s = logit[j % 2]
                nc.tensor.matmul(s[:, :], ident_r[:, :], masks[:, i, :], start=True, stop=False)
                for e in range(2):
                    qb = 2 * i + e
                    k0 = max(qb - 1, 0) * P
                    to = s[:, e * 2 * P + (P if qb == 0 else 0):(e + 1) * 2 * P]
                    qs, ks = slice(qb * P, (qb + 1) * P), slice(k0, (qb + 1) * P)
                    nc.tensor.matmul(to, q1[:, qs], k1[:, ks], start=False, stop=False)
                    mm = nc.tensor.matmul(to, q2[:, qs], k2[:, ks], start=False, stop=e == 1)
                mm.then_inc(s_ready, 1)

            def swa_t(hd, i):
                return SWA_T0 + 2 * hd + i

            def swa_transposes(hd, i):
                j = swa_t(hd, i)
                if i == 0:
                    pe.wait_ge(prob_done, HEADS + hd + 1)
                pe.wait_ge(t_free, j - 1)
                for e in range(2):
                    kb = 2 * i + e
                    for own, qb in ((1, kb), (0, kb + 1)):
                        if qb < NB:
                            c = qb * 2 * P + own * P
                            at = e * 2 * P + (1 - own) * P
                            mm = nc.tensor.transpose(trans[j % 2][:, at:at + P], prob[hd % 2][:, c:c + P], ident[:, :])
                mm.then_inc(t_ready, 1)

            def swa_mix(hd):
                pe.wait_ge(t_free, swa_t(hd, 1) + 1)
                pe.wait_ge(o_done, HEADS + hd - 1)
                o = mix[hd % 2]
                for kb in range(NB):
                    n = P * min(2, NB - kb)
                    for v, t in ((v_hi, pt_hi), (v_hi, pt_lo), (v_lo, pt_hi)):
                        mm = nc.tensor.matmul(o[:, kb * P:kb * P + n], v[:, 0, kb, :], t[:, kb * 2 * P:kb * 2 * P + n],
                                              start=(kb == 0 and v is v_hi and t is pt_hi), skip_group_check=True,
                                              stop=(kb == NB - 1 and v is v_lo))
                mm.then_inc(pv_done, 1)

            swa_proj(0, 0, KT)
            value_transposes(FOX_T, G_SWA + 1)
            for p in range(PAIRS):
                a, b, nxt = 2 * p, 2 * p + 1, p + 1
                swa_proj(nxt, 0, 3)
                swa_logits(a, 0)
                swa_proj(nxt, 3, 4)
                swa_logits(a, 1)
                swa_proj(nxt, 4, 8)
                swa_logits(b, 0)
                swa_transposes(a, 0)
                swa_transposes(a, 1)
                swa_logits(b, 1)
                swa_mix(a)
                swa_transposes(b, 0)
                swa_transposes(b, 1)
                swa_mix(b)

            out_proj(W_SWA_OUT, G_SWA_OUT, 5, HEADS)
            mlp(1, 6)

            for k in range(KT):
                pe.wait_ge(x_done, KT * 4 + k + 1)
                if k >= 2:
                    pe.wait_ge(fin_done, k - 1)
                for b in range(NB):
                    mm = nc.tensor.transpose(trans[k % 2][:, b * P:(b + 1) * P], xT[:, k, b * P:(b + 1) * P],
                                             ident[:, :])
                mm.then_inc(fin_ready, 1)

        @block.scalar
        def _(sc):
            def split(n):
                if n >= W_END:
                    return
                sc.wait_ge(raw_landed[n % RAW], 16 * (n // RAW + 1))
                if n >= RING:
                    sc.wait_ge(used, n - RING + 1)
                nc.scalar.activation(w_hi[:, n % RING, :, :], w_raw[:, n % RAW, :, :], ACT.Copy).then_inc(whi_done, 1)

            def squares(norm, k, src, ready, count):
                sc.wait_ge(ready, count)
                if norm * KT + k >= 2:
                    sc.wait_ge(stat_done, norm * KT + k - 1)
                nc.scalar.activation(tmp[:, k % 2, :], src, ACT.Square).then_inc(sq_done, 1)

            def root(norm):
                sc.wait_ge(ms_done, norm + 1)
                nc.scalar.activation(tmp[:, 3, :], tmp[:, 2, :], ACT.Ln).then_inc(r0_step, 1)
                sc.wait_ge(r0_step, 2 * norm + 1)
                nc.scalar.activation(tmp[:, 3, :], tmp[:, 3, :], ACT.Exp, scale=-0.5).then_inc(r0_step, 1)

            def pre_high(i):
                for k in range(KT):
                    sc.wait_ge(hf_done, i * KT + k + 1)
                    nc.scalar.activation(h_hi[:, k, :], tmp[:, k % 2, :], ACT.Copy).then_inc(hh_done, 1)

            sc.wait_ge(angle_done, 1)
            nc.scalar.activation(sin_t[:, :], tmp[:, 1, :], ACT.Sin, scale=sign[:, 0:1])
            nc.scalar.activation(cos_t[:, :], tmp[:, 2, :], ACT.Sin).then_inc(table_done, 1)
            for n in range(AHEAD):
                split(n)
            sc.wait_ge(const_done, 1)
            nc.scalar.activation(ident_r[:, :], ident[:, :], ACT.Copy)
            nc.scalar.activation(masks[:, :, :], mask_src, ACT.Copy).then_inc(mask_done, 1)
            for k in range(KT):
                squares(0, k, xT[:, k, :], x_done, k + 1)
            root(0)
            pre_high(0)

            split(W_FOX + AHEAD)
            gate_rows = slice(P - 32, P)
            sc.wait_ge(gate_step, 1)
            nc.scalar.activation(tmp[gate_rows, 3, :], tmp[gate_rows, 3, :], ACT.Exp).then_inc(gate_act, 1)
            sc.wait_ge(gate_step, 2)
            nc.scalar.activation(tmp[gate_rows, 0, :], tmp[gate_rows, 0, :], ACT.Ln).then_inc(gate_act, 1)

            def fox_exp(hd, qb):
                j, n = hd * NB + qb, (qb + 1) * P
                sc.wait_ge(max_done, j + 1)
                if hd >= 2 and qb == 0:
                    sc.wait_ge(t_ready, fox_t(hd - 2, 2) + 1)
                nc.scalar.activation(prob[hd % 2][:, FOX_OFF[qb]:FOX_OFF[qb] + n], logit[j % 2][:, 0:n], ACT.Exp,
                                     bias=nmax[:, hd % 2, qb:qb + 1],
                                     accum_out=rsum[:, hd % 2, qb:qb + 1]).then_inc(exp_done, 1)

            def high_q(g, src, q1, q2):
                for side in range(2):
                    h = half(side)
                    nc.scalar.activation(q2[side][h, :], src[h, :], ACT.Copy, scale=SCALE)
                    last = nc.scalar.activation(q1[side][h, :], src[h, :], ACT.Copy, scale=SCALE)
                last.then_inc(hi_done, 1)

            def fox_high_q(p):
                if p == PAIRS:
                    return
                g = G_FOX + 1 + 3 * p
                sc.wait_ge(used, W_FOX + 2 + 3 * p)
                ops = [fox_ops(p, s) for s in range(2)]
                high_q(g, acc[g % 2], [o[0] for o in ops], [o[1] for o in ops])

            def fox_high_k(p):
                if p == PAIRS:
                    return
                g = G_FOX + 2 + 3 * p
                sc.wait_ge(used, W_FOX + 3 + 3 * p)
                for side in range(2):
                    k1 = fox_ops(p, side)[2]
                    for to in range(2):
                        last = nc.scalar.activation(k1[half(to), :], acc[g % 2][half(side), :], ACT.Copy)
                last.then_inc(hi_done, 1)

            def high_v(j, slot):
                sc.wait_ge(t_ready, j + 1)
                nc.scalar.activation(v_hi[:, slot, :, :].rearrange("p b n -> p (b n)"), trans[j % 2][:, :],
                                     ACT.Copy).then_inc(vh_done, 1)

            def high_t(j, at, n, free):
                sc.wait_ge(t_ready, j + 1)
                if free:
                    sc.wait_ge(pv_done, free)
                nc.scalar.activation(pt_hi[:, at:at + n], trans[j % 2][:, 0:n], ACT.Copy).then_inc(th_done, 1)

            def fox_high_t(hd, i):
                high_t(fox_t(hd, i), FOX_PT[i], (512, 384, 384)[i], hd)

            def high_o(hd, rows):
                p, side = divmod(hd % HEADS, 2)
                sc.wait_ge(pv_done, hd + 1)
                nc.scalar.activation(o_hi[half(side), p, :], mix[hd % 2][rows, :], ACT.Copy).then_inc(oh_done, 1)

            t0 = W_FOX + 1
            split(t0 + AHEAD)
            fox_high_q(0)
            split(t0 + AHEAD + 1)
            fox_high_k(0)
            split(t0 + AHEAD + 2)
            for p in range(PAIRS):
                a, b, nxt, t = 2 * p, 2 * p + 1, p + 1, t0 + 3 * (p + 1) + AHEAD
                proj = p + 1 < PAIRS
                fox_exp(a, 0)
                fox_exp(a, 1)
                if proj:
                    split(t)
                high_v(7 * p, p % 2)
                fox_exp(a, 2)
                fox_exp(a, 3)
                fox_exp(b, 0)
                fox_high_q(nxt)
                if proj:
                    split(t + 1)
                fox_exp(b, 1)
                fox_high_t(a, 0)
                fox_high_t(a, 1)
                fox_exp(b, 2)
                fox_high_t(a, 2)
                fox_exp(b, 3)
                fox_high_k(nxt)
                if proj:
                    split(t + 2)
                high_o(a, half(0))
                fox_high_t(b, 0)
                fox_high_t(b, 1)
                fox_high_t(b, 2)
                high_o(b, half(1))

            def out_proj(w0, g0, norm):
                for o in range(KT):
                    split(w0 + o + AHEAD)
                    squares(norm, o, yT[:, o, :], acc_free, g0 + o + 1)
                root(norm)
                for k in range(KT):
                    squares(norm + 1, k, xT[:, k, :], x_done, ((norm + 1) // 2) * KT + k + 1)
                root(norm + 1)
                pre_high((norm + 1) // 2)

            def mlp(layer, norm):
                n, g = W_MLP[layer], G_MLP[layer]
                for c in range(CHUNKS):
                    for j in range(F_CHUNK):
                        split(n + AHEAD)
                        sc.wait_ge(used, n + 1)
                        nc.scalar.activation(tmp[:, j % 2, :], acc[g % 2][:, :], ACT.Relu).then_inc(relu_done, 1)
                        sc.wait_ge(acc_free, g + 1)
                        nc.scalar.activation(u_hi[:, j, :], tmp[:, 2 + j % 2, :], ACT.Copy).then_inc(uhi_done, 1)
                        n, g = n + 1, g + 1
                    for o in range(KT):
                        for hf in range(HALVES):
                            split(n + AHEAD)
                            n += 1
                        g += 1
                        if c == CHUNKS - 1:
                            squares(norm + 1, o, yT[:, o, :], acc_free, g)
                root(norm + 1)

            out_proj(W_FOX_OUT, G_FOX_OUT, 1)
            mlp(0, 2)
            for k in range(KT):
                squares(4, k, xT[:, k, :], x_done, 2 * KT + k + 1)
            root(4)
            pre_high(2)

            def rotate(g, i):
                sc.wait_ge(used, g + 1 + W_SWA - G_SWA)
                for q in range(4):
                    last = nc.scalar.activation(rope[0][32 * (q ^ 1):32 * (q ^ 1) + 32, :],
                                                acc[g % 2][32 * q:32 * q + 32, :], ACT.Copy)
                last.then_inc(rot_done, 1)
                sc.wait_ge(rope_done, i + 1)

            def swa_high_k():
                rotate(G_SWA, 0)
                for kv in range(2):
                    k1 = swa_k(kv, 0)[0]
                    for to in range(2):
                        last = nc.scalar.activation(k1[half(to), :], rope[2][half(kv), :], ACT.Copy)
                last.then_inc(hi_done, 1)

            def swa_high_q(p):
                if p == PAIRS:
                    return
                g = G_SWA + 2 + p
                rotate(g, 1 + p)
                ops = [swa_q(p, s) for s in range(2)]
                high_q(g, rope[2], [o[0] for o in ops], [o[1] for o in ops])

            def swa_exp(hd, i):
                j = FOX_S + hd * 2 + i
                sc.wait_ge(max_done, j + 1)
                if i == 0:
                    if hd >= 2:
                        sc.wait_ge(t_ready, SWA_T0 + 2 * (hd - 2) + 2)
                for e in range(2):
                    qb = 2 * i + e
                    last = nc.scalar.activation(prob[hd % 2][:, qb * 2 * P:(qb + 1) * 2 * P],
                                                logit[j % 2][:, e * 2 * P:(e + 1) * 2 * P], ACT.Exp,
                                                bias=nmax[:, hd % 2, qb:qb + 1],
                                                accum_out=rsum[:, hd % 2, qb:qb + 1])
                last.then_inc(exp_done, 1)
                if i == 1:
                    nc.scalar.activation(esink[:, hd % 2, :], nmax[:, hd % 2, :], ACT.Exp,
                                         bias=sinks[:, hd:hd + 1]).then_inc(es_done, 1)

            def swa_high_t(hd, i):
                high_t(SWA_T0 + 2 * hd + i, i * 512, (512, 384)[i], HEADS + hd)

            split(W_SWA + AHEAD)
            swa_high_k()
            split(W_SWA + 1 + AHEAD)
            split(W_SWA + 2 + AHEAD)
            swa_high_q(0)
            high_v(FOX_T, 0)
            for p in range(PAIRS):
                a, b, nxt = 2 * p, 2 * p + 1, p + 1
                if nxt < PAIRS:
                    split(W_SWA + 2 + nxt + AHEAD)
                swa_exp(a, 0)
                swa_exp(a, 1)
                swa_high_q(nxt)
                swa_exp(b, 0)
                swa_high_t(a, 0)
                swa_high_t(a, 1)
                swa_exp(b, 1)
                high_o(HEADS + a, half(a // GROUP))
                swa_high_t(b, 0)
                swa_high_t(b, 1)
                high_o(HEADS + b, half(b // GROUP))

            out_proj(W_SWA_OUT, G_SWA_OUT, 5)
            mlp(1, 6)

        @block.vector
        def _(ve):
            steps = [0]

            def own(ins):
                steps[0] += 1
                ins.then_inc(dve_step, 1)
                ve.wait_ge(dve_step, steps[0])

            f32 = lambda ap: ap.bitcast(F32)

            def split(n):
                if n >= W_END:
                    return
                ve.wait_ge(whi_done, n + 1)
                nc.vector.tensor_tensor(w_lo[:, n % RING, :, :], w_raw[:, n % RAW, :, :],
                                        f32(w_hi[:, n % RING, :, :]), ALU.subtract).then_inc(wlo_done, 1)

            def root(norm):
                ve.wait_ge(stat_done, (norm + 1) * KT)
                nc.vector.tensor_scalar(tmp[:, 2, :], mix[norm % 2][:, :], 1.0 / D, EPS, ALU.mult,
                                        ALU.add).then_inc(ms_done, 1)
                ve.wait_ge(r0_step, 2 * norm + 2)
                own(nc.vector.scalar_tensor_tensor(tmp[:, 2, :], tmp[:, 2, :], -0.5, tmp[:, 3, :], ALU.mult, ALU.mult))
                own(nc.vector.tensor_tensor(tmp[:, 2, :], tmp[:, 2, :], tmp[:, 3, :], ALU.mult))
                own(nc.vector.scalar_tensor_tensor(rstd[:, :], tmp[:, 2, :], 1.5, tmp[:, 3, :], ALU.add, ALU.mult))

            def post(kind, layer, norm):
                root(norm)
                for k in range(KT):
                    own(nc.vector.scalar_tensor_tensor(tmp[:, 2 + k % 2, :], yT[:, k, :],
                                                       gains[:, kind, layer, k:k + 1], rstd[:, :], ALU.mult, ALU.mult))
                    nc.vector.tensor_tensor(xT[:, k, :], xT[:, k, :], tmp[:, 2 + k % 2, :],
                                            ALU.add).then_inc(x_done, 1)

            def pre(kind, layer, norm):
                root(norm)
                base = norm // 2 * KT

                def low(k):
                    ve.wait_ge(hh_done, base + k + 1)
                    nc.vector.tensor_tensor(h_lo[:, k, :], tmp[:, k % 2, :], f32(h_hi[:, k, :]),
                                            ALU.subtract).then_inc(h_done, 1)
                for k in range(KT):
                    if k >= 2:
                        low(k - 2)
                        ve.wait_ge(h_done, base + k - 1)
                    nc.vector.scalar_tensor_tensor(tmp[:, k % 2, :], xT[:, k, :], gains[:, kind, layer, k:k + 1],
                                                   rstd[:, :], ALU.mult, ALU.mult).then_inc(hf_done, 1)
                low(KT - 2)
                low(KT - 1)

            def gates():
                r = slice(P - 32, P)
                z, e, u, c = (tmp[r, i, :] for i in (1, 3, 0, 2))
                ve.wait_ge(used, W_FOX + 1)
                nc.vector.tensor_scalar(z, acc[G_FOX % 2][r, :], b_f[r, 0:1], None, ALU.add).then_inc(acc_free, 1)
                ve.wait_ge(acc_free, G_FOX + 1)
                nc.vector.scalar_tensor_tensor(e, z, -1.0, z, ALU.mult, ALU.min).then_inc(gate_step, 1)
                ve.wait_ge(gate_act, 1)
                own(nc.vector.tensor_scalar(u, e, 1.0, None, ALU.add))
                own(nc.vector.scalar_tensor_tensor(e, u, -1.0, e, ALU.add, ALU.subtract))
                nc.vector.memset(c, 0.0).then_inc(gate_step, 1)
                ve.wait_ge(gate_act, 2)
                own(nc.vector.tensor_tensor(u, u, e, ALU.subtract))
                own(nc.vector.scalar_tensor_tensor(z, z, 0.0, u, ALU.min, ALU.subtract))
                own(nc.vector.tensor_tensor_scan(e, z, c, 0.0, ALU.add, ALU.add))
                own(nc.vector.tensor_copy(pt_hi[r, 0:SEQ], e))
                nc.vector.tensor_tensor(pt_lo[r, 0:SEQ], e, f32(pt_hi[r, 0:SEQ]), ALU.subtract).then_inc(c_done, 1)

            def low_q(src, q1, end):
                for side in range(2):
                    last = nc.vector.scalar_tensor_tensor(q1[side][half(1 - side), :], src[half(side), :], SCALE,
                                                          f32(q1[side][half(side), :]), ALU.mult, ALU.subtract)
                last.then_inc(end, 1)

            def fox_low_q(p):
                ve.wait_ge(hi_done, 2 * p + 1)
                low_q(acc[(G_FOX + 1 + 3 * p) % 2], [fox_ops(p, s)[0] for s in range(2)], acc_free)

            def fox_low_k(p):
                ve.wait_ge(hi_done, 2 * p + 2)
                for side in range(2):
                    _, _, k1, k2 = fox_ops(p, side)
                    h = half(side)
                    last = nc.vector.tensor_tensor(k2[h, :], acc[(G_FOX + 2 + 3 * p) % 2][h, :], f32(k1[h, :]),
                                                   ALU.subtract)
                last.then_inc(acc_free, 1)

            def value_copy(n, g):
                ve.wait_ge(used, n + 1)
                nc.vector.tensor_copy(tmp[:, 0, :], acc[g % 2][:, :]).then_inc(acc_free, 1)

            def low_v(j, slot, i):
                ve.wait_ge(vh_done, i + 1)
                nc.vector.tensor_tensor(v_lo[:, slot, :, :].rearrange("p b n -> p (b n)"), trans[j % 2][:, :],
                                        f32(v_hi[:, slot, :, :].rearrange("p b n -> p (b n)")),
                                        ALU.subtract).then_inc(t_free, 1)

            def low_t(i, j, at, n):
                ve.wait_ge(th_done, i + 1)
                nc.vector.tensor_tensor(pt_lo[:, at:at + n], trans[j % 2][:, 0:n], f32(pt_hi[:, at:at + n]),
                                        ALU.subtract).then_inc(t_free, 1)

            def fox_low_t(hd, i):
                low_t(3 * hd + i, fox_t(hd, i), FOX_PT[i], (512, 384, 384)[i])

            def swa_low_t(hd, i):
                low_t(3 * HEADS + 2 * hd + i, SWA_T0 + 2 * hd + i, i * 512, (512, 384)[i])

            def low_o(hd, rows):
                p, side = divmod(hd % HEADS, 2)
                ve.wait_ge(oh_done, hd + 1)
                nc.vector.tensor_tensor(o_lo[half(side), p, :], mix[hd % 2][rows, :], f32(o_hi[half(side), p, :]),
                                        ALU.subtract).then_inc(o_done, 1)

            def fox_max(hd, qb):
                j = hd * NB + qb
                ve.wait_ge(s_ready, j + 1)
                nc.vector.reduce_max(nmax[:, hd % 2, qb:qb + 1], logit[j % 2][:, 0:(qb + 1) * P], AX_X,
                                     negate=True).then_inc(max_done, 1)

            def fox_norm(hd):
                ve.wait_ge(exp_done, (hd + 1) * NB)
                own(nc.vector.reciprocal(rden[:, hd % 2, :], rsum[:, hd % 2, :]))
                for qb in range(NB):
                    pr = prob[hd % 2][:, FOX_OFF[qb]:FOX_OFF[qb] + (qb + 1) * P]
                    last = nc.vector.tensor_scalar(pr, pr, rden[:, hd % 2, qb:qb + 1], None, ALU.mult)
                last.then_inc(prob_done, 1)

            def swa_max(hd, i):
                j = FOX_S + hd * 2 + i
                ve.wait_ge(s_ready, j + 1)
                nm = nmax[:, hd % 2, 2 * i:2 * i + 2]
                own(nc.vector.reduce_max(nm, logit[j % 2][:, :].rearrange("p (e n) -> p e n", e=2), AX_X, negate=True))
                nc.vector.tensor_scalar(nm, nm, nsinks[:, hd:hd + 1], None, ALU.min).then_inc(max_done, 1)

            def swa_norm(hd):
                ve.wait_ge(es_done, hd + 1)
                own(nc.vector.tensor_tensor(rden[:, hd % 2, :], rsum[:, hd % 2, :], esink[:, hd % 2, :], ALU.add))
                own(nc.vector.reciprocal(rden[:, hd % 2, :], rden[:, hd % 2, :]))
                for qb in range(NB):
                    pr = prob[hd % 2][:, qb * 2 * P:(qb + 1) * 2 * P]
                    last = nc.vector.tensor_scalar(pr, pr, rden[:, hd % 2, qb:qb + 1], None, ALU.mult)
                last.then_inc(prob_done, 1)

            def rotate(g, i):
                ve.wait_ge(rot_done, i + 1)
                nc.vector.tensor_tensor(rope[1], acc[g % 2][:, :], cos_t[:, :], ALU.mult).then_inc(acc_free, 1)
                own(nc.vector.tensor_tensor(rope[0], rope[0], sin_t[:, :], ALU.mult))
                nc.vector.tensor_tensor(rope[2], rope[0], rope[1], ALU.add).then_inc(rope_done, 1)

            def swa_low_k():
                ve.wait_ge(hi_done, 2 * PAIRS + 1)
                for kv in range(KV_HEADS):
                    for side in range(2):
                        k1, k2 = swa_k(kv, side)
                        last = nc.vector.tensor_tensor(k2[half(side), :], rope[2][half(kv), :], f32(k1[half(kv), :]),
                                                       ALU.subtract)
                last.then_inc(q_done, 1)

            def swa_low_q(p):
                rotate(G_SWA + 2 + p, 1 + p)
                ve.wait_ge(hi_done, 2 * PAIRS + 2 + p)
                low_q(rope[2], [swa_q(p, s)[0] for s in range(2)], q_done)

            def out_proj(w0, g0):
                for o in range(KT):
                    split(w0 + o + AHEAD)
                    ve.wait_ge(used, w0 + o + 1)
                    nc.vector.tensor_copy(yT[:, o, :], acc[(g0 + o) % 2][:, :]).then_inc(acc_free, 1)

            def mlp(layer):
                n, g = W_MLP[layer], G_MLP[layer]
                for c in range(CHUNKS):
                    for j in range(F_CHUNK):
                        split(n + AHEAD)
                        i = (layer * CHUNKS + c) * F_CHUNK + j
                        ve.wait_ge(relu_done, i + 1)
                        nc.vector.tensor_tensor(tmp[:, 2 + j % 2, :], acc[g % 2][:, :], tmp[:, j % 2, :],
                                                ALU.mult).then_inc(acc_free, 1)
                        ve.wait_ge(uhi_done, i + 1)
                        nc.vector.tensor_tensor(u_lo[:, j, :], tmp[:, 2 + j % 2, :], f32(u_hi[:, j, :]),
                                                ALU.subtract).then_inc(u_done, 1)
                        n, g = n + 1, g + 1
                    for o in range(KT):
                        for _ in range(HALVES):
                            split(n + AHEAD)
                            n += 1
                        ve.wait_ge(used, n)
                        if c == 0:
                            nc.vector.tensor_copy(yT[:, o, :], acc[g % 2][:, :]).then_inc(acc_free, 1)
                        else:
                            nc.vector.tensor_tensor(yT[:, o, :], acc[g % 2][:, :], yT[:, o, :],
                                                    ALU.add).then_inc(acc_free, 1)
                        g += 1

            ve.wait_ge(pos_landed, 16)
            ve.wait_ge(freq_t, 1)
            nc.vector.tensor_copy(tmp[:, 0, :], tmp[:, 3, :].bitcast(I32))
            own(nc.vector.tensor_copy(freq[:, :], mix[1][:, 0:1]))
            own(nc.vector.tensor_scalar(tmp[:, 1, :], tmp[:, 0, :], freq[:, 0:1], None, ALU.mult))
            magic = 1.5 * 2.0 ** 23
            own(nc.vector.tensor_scalar(tmp[:, 0, :], tmp[:, 1, :], 0.5 / np.pi, magic, ALU.mult, ALU.add))
            own(nc.vector.tensor_scalar(tmp[:, 0, :], tmp[:, 0, :], -magic, None, ALU.add))
            for part in two_pi_parts():
                own(nc.vector.scalar_tensor_tensor(tmp[:, 1, :], tmp[:, 0, :], -part, tmp[:, 1, :], ALU.mult, ALU.add))
            PI = 3.1415925
            own(nc.vector.tensor_scalar(tmp[:, 1, :], tmp[:, 1, :], PI, -PI, ALU.min, ALU.max))
            own(nc.vector.tensor_scalar(tmp[:, 2, :], tmp[:, 1, :], np.pi / 2, None, ALU.add))
            own(nc.vector.tensor_scalar(tmp[:, 0, :], tmp[:, 2, :], PI, -2 * np.pi, ALU.is_gt, ALU.mult))
            own(nc.vector.tensor_tensor(tmp[:, 2, :], tmp[:, 2, :], tmp[:, 0, :], ALU.add))
            nc.vector.tensor_scalar(tmp[:, 2, :], tmp[:, 2, :], PI, -PI, ALU.min, ALU.max).then_inc(angle_done, 1)
            ve.wait_ge(table_done, 1)

            ve.wait_ge(small_landed, 16 * 10)
            own(nc.vector.tensor_scalar(nsinks[:, :], sinks[:, :], -1.0, None, ALU.mult))
            for n in range(AHEAD):
                split(n)
            for k in range(KT):
                ve.wait_ge(xt_ready, k + 1)
                nc.vector.tensor_copy(xT[:, k, :], trans[k % 2][:, :]).then_inc(x_done, 1)

            pre(0, 0, 0)

            split(W_FOX + AHEAD)
            gates()
            t0 = W_FOX + 1
            split(t0 + AHEAD)
            fox_low_q(0)
            split(t0 + AHEAD + 1)
            fox_low_k(0)
            split(t0 + AHEAD + 2)
            value_copy(W_FOX + 3, G_FOX + 3)
            for p in range(PAIRS):
                a, b, nxt, t = 2 * p, 2 * p + 1, p + 1, t0 + 3 * (p + 1) + AHEAD
                proj = nxt < PAIRS
                fox_max(a, 0)
                fox_max(a, 1)
                if proj:
                    split(t)
                low_v(7 * p, p % 2, p)
                fox_max(a, 2)
                fox_max(a, 3)
                fox_max(b, 0)
                fox_norm(a)
                if proj:
                    fox_low_q(nxt)
                    split(t + 1)
                fox_max(b, 1)
                fox_low_t(a, 0)
                fox_low_t(a, 1)
                fox_max(b, 2)
                fox_low_t(a, 2)
                fox_max(b, 3)
                fox_norm(b)
                if proj:
                    fox_low_k(nxt)
                    split(t + 2)
                low_o(a, half(0))
                fox_low_t(b, 0)
                fox_low_t(b, 1)
                fox_low_t(b, 2)
                if proj:
                    value_copy(W_FOX + 3 + 3 * nxt, G_FOX + 3 + 3 * nxt)
                low_o(b, half(1))

            out_proj(W_FOX_OUT, G_FOX_OUT)
            post(1, 0, 1)
            pre(2, 0, 2)
            mlp(0)
            post(3, 0, 3)
            pre(0, 1, 4)

            split(W_SWA + AHEAD)
            rotate(G_SWA, 0)
            swa_low_k()
            split(W_SWA + 1 + AHEAD)
            value_copy(W_SWA + 1, G_SWA + 1)
            split(W_SWA + 2 + AHEAD)
            swa_low_q(0)
            low_v(FOX_T, 0, PAIRS)
            for p in range(PAIRS):
                a, b, nxt = 2 * p, 2 * p + 1, p + 1
                if nxt < PAIRS:
                    split(W_SWA + 2 + nxt + AHEAD)
                swa_max(a, 0)
                swa_max(a, 1)
                swa_norm(a)
                if nxt < PAIRS:
                    swa_low_q(nxt)
                swa_max(b, 0)
                swa_low_t(a, 0)
                swa_low_t(a, 1)
                swa_max(b, 1)
                swa_norm(b)
                low_o(HEADS + a, half(a // GROUP))
                swa_low_t(b, 0)
                swa_low_t(b, 1)
                low_o(HEADS + b, half(b // GROUP))

            out_proj(W_SWA_OUT, G_SWA_OUT)
            post(1, 1, 5)
            pre(2, 1, 6)
            mlp(1)
            post(3, 1, 7)
            for k in range(KT):
                ve.wait_ge(fin_ready, k + 1)
                nc.vector.tensor_copy(yT[:, k, :], trans[k % 2][:, :]).then_inc(fin_done, 1)


_INS = ["x", "positions", "fox_w_in", "fox_b_f", "fox_w_out", "swa_w_in", "swa_sinks", "swa_w_out",
        "norm_pre_mix", "norm_post_mix", "norm_pre_ffn", "norm_post_ffn", "mlp_w_up", "mlp_w_down"]


def kernel(**inputs):
    import numpy as _np
    import concourse.bacc as _bacc
    from concourse import mybir as _mybir
    from concourse.bass_utils import run_bass_kernel_spmd as _run

    nc = _bacc.Bacc("TRN2", target_bir_lowering=False, num_devices=1)
    arrays, args = {}, []
    for name in _INS:
        a = _np.ascontiguousarray(inputs[name])
        arrays[f"in_{name}_dram"] = a
        args.append(nc.dram_tensor(f"in_{name}_dram", a.shape, _mybir.dt.from_np(a.dtype), kind="ExternalInput").ap())
    args.append(nc.dram_tensor("out_0_dram", (1, SEQ, D), F32, kind="ExternalOutput").ap())
    trunk(nc, *args)
    r = _run(nc, [arrays], core_ids=[0])
    return r.results[0]["out_0_dram"]
```

```python
from contextlib import ExitStack

import numpy as np

import concourse.bass as bass
from concourse import mybir

F32 = mybir.dt.float32
F32R = mybir.dt.float32r
I32 = mybir.dt.int32
ALU = mybir.AluOpType
ACT = mybir.ActivationFunctionType
AX_X = mybir.AxisListType.X

P = 128
SEQ = 512
D = 1024
D_FF = 4096
HD = 64
HEADS = 16
KV_HEADS = 2
GROUP = HEADS // KV_HEADS
NB = SEQ // P
KT = D // P
PAIRS = HEADS // 2
QD = HEADS * HD
KVD = KV_HEADS * HD
FOX_IN = 3 * QD + HEADS
EPS = 1e-6
SCALE = HD ** -0.5
NEG = -1e30
ROPE_THETA = 10000.0

RING = 4
RAW = 2
AHEAD = RING - 1

F_CHUNK = 16
CHUNKS = D_FF // P // F_CHUNK
HALVES = F_CHUNK // KT

W_FOX = 0
W_FOX_OUT = W_FOX + 1 + 3 * PAIRS
W_MLP = [W_FOX_OUT + KT, 0]
MLP_TILES = CHUNKS * (F_CHUNK + KT * HALVES)
W_SWA = W_MLP[0] + MLP_TILES
W_SWA_OUT = W_SWA + 2 + PAIRS
W_MLP[1] = W_SWA_OUT + KT
W_END = W_MLP[1] + MLP_TILES
G_FOX = 0
G_FOX_OUT = G_FOX + 1 + 3 * PAIRS
G_MLP = [G_FOX_OUT + KT, 0]
MLP_GROUPS = CHUNKS * (F_CHUNK + KT)
G_SWA = G_MLP[0] + MLP_GROUPS
G_SWA_OUT = G_SWA + 2 + PAIRS
G_MLP[1] = G_SWA_OUT + KT

EARLY = 6

TABLE_SLOT = HEADS - 1

FOX_OFF = [0, 128, 384, 768]
FOX_PT = [0, 512, 896, 1152]
FOX_P = 1280
SWA_P = NB * 2 * P


def inv_freq():
    return np.float32(1) / (ROPE_THETA ** (np.arange(0, HD, 2) / HD)).astype(np.float32)


def two_pi_parts():
    rest, parts = 2 * np.pi, []
    for _ in range(5):
        step = 2.0 ** (np.floor(np.log2(rest)) - 5)
        parts.append(float(np.floor(rest / step) * step))
        rest -= parts[-1]
    return parts + [float(np.float32(rest))]


def trunk(nc, x, positions, fox_w_in, fox_b_f, fox_w_out, swa_w_in, swa_sinks, swa_w_out,
          norm_pre_mix, norm_post_mix, norm_pre_ffn, norm_post_ffn, mlp_w_up, mlp_w_down, out):
    with ExitStack() as ctx:
        def sb(name, shape, dt=F32):
            return ctx.enter_context(nc.sbuf_tensor(name, shape, dt))

        def sem(name):
            return ctx.enter_context(nc.semaphore(name))

        xT = sb("xT", [P, KT, SEQ])
        yT = sb("yT", [P, KT, SEQ])
        h_hi = sb("h_hi", [P, KT, SEQ], F32R)
        h_lo = sb("h_lo", [P, KT, SEQ], F32R)
        w_raw = sb("w_raw", [P, RAW, KT, P])
        w_hi = sb("w_hi", [P, RING, KT, P], F32R)
        w_lo = sb("w_lo", [P, RING, KT, P], F32R)
        act = sb("act", [P, 32, SEQ], F32R)
        pt_hi = sb("pt_hi", [P, FOX_P], F32R)
        pt_lo = sb("pt_lo", [P, FOX_P], F32R)
        v_hi = sb("v_hi", [P, 2, NB, P], F32R)
        v_lo = sb("v_lo", [P, 2, NB, P], F32R)
        tmp = sb("tmp", [P, 4, SEQ])
        rstd = sb("rstd", [P, SEQ])
        cos_t = sb("cos_t", [P, SEQ])
        sin_t = sb("sin_t", [P, SEQ])
        ident = sb("ident", [P, P])
        ones = sb("ones", [P, P])
        ident_r = sb("ident_r", [P, P], F32R)
        masks = sb("masks", [P, 2, 4 * P], F32R)
        gains = sb("gains", [P, 4, 2, KT])
        freq_row = sb("freq_row", [1, P])
        freq = sb("freq", [P, 1])
        sign = sb("sign", [P, 1])
        eps = sb("eps", [P, 1])
        b_f = sb("b_f", [P, 1])
        sinks = sb("sinks", [P, HEADS])
        nsinks = sb("nsinks", [P, HEADS])
        pool_flag = sb("pool_flag", [P, 1])
        nmax = sb("nmax", [P, 2, NB])
        rsum = sb("rsum", [P, 2, NB])
        esink = sb("esink", [P, 2, NB])
        rden = sb("rden", [P, 2, NB])

        o_hi, o_lo = act[:, 0:8, :], act[:, 8:16, :]
        u_hi, u_lo = act[:, 0:F_CHUNK, :], act[:, F_CHUNK:2 * F_CHUNK, :]
        y_flat = yT[:, :, :].rearrange("p k t -> p (k t)")
        prob = [y_flat[:, h * FOX_P:(h + 1) * FOX_P] for h in range(2)]
        rope = [y_flat[:, (5 + i) * SEQ:(6 + i) * SEQ] for i in range(3)]
        unrotated = [tmp[:, 1, :], tmp[:, 2, :]]
        swapped = [rope[0], tmp[:, 3, :]]
        x_in = y_flat.rearrange("p (b d) -> p b d", b=NB)
        mask_src = xT[:, KT - 2:KT, :]

        def fox_ops(p, side):
            s = 16 + 8 * (p % 2) + 4 * side
            return act[:, s, :], act[:, s + 1, :], act[:, s + 2, :], act[:, s + 3, :]

        def swa_q(p, side):
            s = 16 + 3 * (p % 2)
            return act[:, s + side, :], act[:, s + 2, :]

        def swa_k(kv, side):
            return act[:, 24 + kv, :], act[:, 26 + 2 * kv + side, :]

        def half(side):
            return slice(HD * side, HD * side + HD)

        def bank(name):
            return ctx.enter_context(nc.psum_tensor(name, [P, SEQ], F32))

        acc = [bank(f"acc{i}") for i in range(2)]
        logit = [bank(f"logit{i}") for i in range(2)]
        mlp_acc = acc + logit
        trans = [bank(f"trans{i}") for i in range(2)]
        mix = [bank(f"mix{i}") for i in range(2)]

        c_dram = nc.dram_tensor("c_scratch", (HEADS, 2, SEQ), F32R).ap()

        raw_landed = [sem(f"raw_landed{i}") for i in range(RAW)]
        whi_done = sem("whi_done")
        wlo_done = sem("wlo_done")
        used = sem("used")
        acc_free = sem("acc_free")
        x_landed = sem("x_landed")
        small_landed = sem("small_landed")
        pos_landed = sem("pos_landed")
        pool_step = sem("pool_step")
        ident_done = sem("ident_done")
        const_done = sem("const_done")
        mask_done = sem("mask_done")
        freq_t = sem("freq_t")
        freq_done = sem("freq_done")
        angle_done = sem("angle_done")
        table_done = sem("table_done")
        xt_ready = sem("xt_ready")
        x_done = sem("x_done")
        sq_done = sem("sq_done")
        stat_done = sem("stat_done")
        ssq_done = sem("ssq_done")
        eps_set = sem("eps_set")
        r0_step = sem("r0_step")
        rstd_done = sem("rstd_done")
        hf_done = sem("hf_done")
        hh_done = sem("hh_done")
        h_done = sem("h_done")
        yn_done = sem("yn_done")
        dve_step = sem("dve_step")
        squared = sem("squared")
        uhi_done = sem("uhi_done")
        u_done = sem("u_done")
        gate_step = sem("gate_step")
        gate_act = sem("gate_act")
        c_done = sem("c_done")
        c_stored = sem("c_stored")
        aug_set = sem("aug_set")
        aug_landed = [sem(f"aug_landed{i}") for i in range(2)]
        swap_landed = [sem(f"swap_landed{i}") for i in range(2)]
        q_copied = [sem(f"q_copied{i}") for i in range(2)]
        q_done = sem("q_done")
        hi_done = sem("hi_done")
        vh_done = sem("vh_done")
        s_ready = sem("s_ready")
        max_done = sem("max_done")
        exp_done = sem("exp_done")
        prob_done = sem("prob_done")
        t_ready = sem("t_ready")
        th_done = sem("th_done")
        t_free = sem("t_free")
        pv_done = sem("pv_done")
        oh_done = sem("oh_done")
        o_done = sem("o_done")
        rot_done = sem("rot_done")
        rope_done = sem("rope_done")
        v_scaled = sem("v_scaled")
        es_done = sem("es_done")
        fin_ready = sem("fin_ready")
        fin_done = sem("fin_done")
        stored = sem("stored")

        def group_bank(g):
            for base in G_MLP:
                if base <= g < base + MLP_GROUPS:
                    return mlp_acc[(g - base) % len(mlp_acc)]
            return acc[g % 2]

        def groups_before(g):
            for base in G_MLP:
                if base <= g < base + MLP_GROUPS:
                    return max(base, g + 1 - len(mlp_acc))
            return g - 1

        def stats_before(norm):
            return norm // 2 * (KT + 2) + norm % 2 * KT

        block = ctx.enter_context(nc.Block())

        def fox_t(hd, i):
            return 7 * (hd // 2) + 1 + 3 * (hd % 2) + i

        FOX_S, FOX_T = HEADS * NB, PAIRS * 7
        SWA_T0 = FOX_T + 1

        @block.sync
        def _(sp):
            xr = x.rearrange("a (b p) d -> p (a b) d", p=P)
            for b in range(NB):
                sp.dma_start(x_in[:, b, :], xr[:, b, :]).then_inc(x_landed, 16)

            def load(n, src):
                if n >= RAW:
                    sp.wait_ge(wlo_done, n - RAW + 1)
                sp.dma_start(w_raw[:, n % RAW, :, :],
                             src.rearrange("(k p) n -> p k n", p=P)).then_inc(raw_landed[n % RAW], 16)

            w_in = fox_w_in[0]
            load(W_FOX, w_in[:, FOX_IN - P:FOX_IN])
            for p in range(PAIRS):
                for j in range(3):
                    load(W_FOX + 1 + 3 * p + j, w_in[:, j * QD + p * P:j * QD + (p + 1) * P])
            for o in range(KT):
                load(W_FOX_OUT + o, fox_w_out[0][:, o * P:(o + 1) * P])

            def load_mlp(layer):
                n = W_MLP[layer]
                for c in range(CHUNKS):
                    for j in range(F_CHUNK):
                        f = (c * F_CHUNK + j) * P
                        load(n, mlp_w_up[layer][:, f:f + P])
                        n += 1
                    for o in range(KT):
                        for hf in range(HALVES):
                            f = (c * F_CHUNK + hf * KT) * P
                            load(n, mlp_w_down[layer][f:f + KT * P, o * P:(o + 1) * P])
                            n += 1

            load_mlp(0)
            w_in2 = swa_w_in[0]
            load(W_SWA, w_in2[:, QD + KVD:QD + 2 * KVD])
            load(W_SWA + 1, w_in2[:, QD:QD + KVD])
            for p in range(PAIRS):
                load(W_SWA + 2 + p, w_in2[:, p * P:(p + 1) * P])
            for o in range(KT):
                load(W_SWA_OUT + o, swa_w_out[0][:, o * P:(o + 1) * P])
            load_mlp(1)

            outr = out.rearrange("a (b p) (k f) -> k p (a b) f", p=P, f=P)
            for k in range(KT):
                sp.wait_ge(fin_done, k + 1)
                sp.dma_start(outr[k], yT[:, k, :].rearrange("p (b f) -> p b f", b=NB)).then_inc(stored, 16)
            sp.wait_ge(stored, 16 * KT)

        @block.gpsimd
        def _(pool):
            step = [0]

            def done(ins):
                step[0] += 1
                ins.then_inc(pool_step, 1)
                pool.wait_ge(pool_step, step[0])

            done(nc.gpsimd.memset(ident[:, :], 0.0))
            done(nc.gpsimd.affine_select(out=ident[:, :], in_=ident[:, :], compare_op=ALU.not_equal, fill=1.0,
                                         base=0, pattern=[[-1, P]], channel_multiplier=1))
            done(nc.gpsimd.memset(b_f[:, :], 0.0))
            nc.gpsimd.memset(ones[:, :], 1.0).then_inc(ident_done, 1)
            pool.wait_ge(ident_done, 1)
            for i, f in enumerate(inv_freq()):
                last = nc.gpsimd.memset(freq_row[0:1, :].rearrange("a (q i) -> a q i", i=HD // 2)[:, :, i], float(f))
            done(last)
            done(nc.gpsimd.memset(sign[:, :], 1.0))
            done(nc.gpsimd.memset(sign[0:32, :], -1.0))
            done(nc.gpsimd.memset(sign[64:96, :], -1.0))
            done(nc.gpsimd.memset(mask_src, 0.0))
            done(nc.gpsimd.memset(mask_src[:, 0, 0:P], NEG))
            for a, at, causal in ((0, 1, 1), (0, 2, 0), (0, 3, 1), (1, 0, 0), (1, 1, 1), (1, 2, 0), (1, 3, 1)):
                m = mask_src[:, a, at * P:(at + 1) * P]
                sgn = 1 if causal else -1
                done(nc.gpsimd.affine_select(out=m, in_=m, compare_op=ALU.is_ge if causal else ALU.is_gt, fill=NEG,
                                             base=0, pattern=[[-sgn, P]], channel_multiplier=sgn))
            nc.gpsimd.memset(pool_flag[:, :], 0.0).then_inc(const_done, 1)
            pool.wait_ge(const_done, 1)

            pool.wait_ge(xt_ready, KT)
            pool.dma_start(rope[2].bitcast(I32), positions.broadcast_to([P, SEQ])).then_inc(pos_landed, 16)

            for p in range(2):
                for side in range(2):
                    _, q2, _, k2 = fox_ops(p, side)
                    o = HD * (1 - side)
                    done(nc.gpsimd.memset(q2[half(1 - side), :].bitcast(F32), 0.0))
                    done(nc.gpsimd.memset(k2[half(1 - side), :].bitcast(F32), 0.0))
                    done(nc.gpsimd.memset(q2[o:o + 4, :].bitcast(F32), -1.0))
                    done(nc.gpsimd.memset(k2[o:o + 4, :].bitcast(F32), 1.0))
            pool.wait_ge(c_done, 1)
            pool.dma_start(c_dram[:, 0, :], pt_hi[P - HEADS:P, 0:SEQ]).then_inc(c_stored, 16)
            pool.dma_start(c_dram[:, 1, :], pt_lo[P - HEADS:P, 0:SEQ]).then_inc(c_stored, 16)
            pool.wait_ge(c_stored, 32)
            for p in range(PAIRS):
                if p >= 2:
                    pool.wait_ge(s_ready, 2 * NB * (p - 1))
                for side in range(2):
                    _, q2, _, k2 = fox_ops(p, side)
                    o = HD * (1 - side)
                    pool.dma_start(q2[o:o + 2, :], c_dram[2 * p + side]).then_inc(aug_landed[p % 2], 16)
                    pool.dma_start(k2[o + 2:o + 4, :], c_dram[2 * p + side]).then_inc(aug_landed[p % 2], 16)
                pool.wait_ge(hi_done, 2 * p + 1)
                for side in range(2):
                    q1, q2, _, _ = fox_ops(p, side)
                    pool.dma_start(q2[half(side), :], q1[half(side), :]).then_inc(aug_landed[p % 2], 16)
                pool.wait_ge(hi_done, 2 * p + 2)
                for side in range(2):
                    k1 = fox_ops(p, side)[2]
                    pool.dma_start(k1[half(1 - side), :], k1[half(side), :]).then_inc(aug_landed[p % 2], 16)

            pool.wait_ge(used, W_SWA)
            for kv in range(KV_HEADS):
                for side in range(2):
                    done(nc.gpsimd.memset(swa_k(kv, side)[1][half(1 - side), :].bitcast(F32), 0.0))
            nc.gpsimd.memset(pool_flag[:, :], 0.0).then_inc(aug_set, 1)

            def swap(i):
                pool.wait_ge(rot_done, i + 1)
                if i >= 2:
                    pool.wait_ge(rope_done, i - 1)
                for q in range(4):
                    pool.dma_start(swapped[i % 2][32 * (q ^ 1):32 * (q ^ 1) + 32, :],
                                   unrotated[i % 2][32 * q:32 * q + 32, :]).then_inc(swap_landed[i % 2], 16)

            def copy_q(p):
                pool.wait_ge(hi_done, 2 * PAIRS + 2 + p)
                for side in range(2):
                    q1, q2 = swa_q(p, side)
                    pool.dma_start(q1[half(side), :], q2[half(side), :]).then_inc(q_copied[p % 2], 16)

            swap(0)
            swap(1)
            swap(2)
            copy_q(0)
            copy_q(1)
            for p in range(2, PAIRS):
                swap(1 + p)
                copy_q(p)

        @block.tensor
        def _(pe):
            def project(n, g, rhs_hi, rhs_lo, k0=0, k1=KT, first=True, last=True, rhs_ready=None, starts=True):
                if k0 == 0 and starts:
                    pe.wait_ge(wlo_done, n + 1)
                    if first and g >= 2:
                        pe.wait_ge(acc_free, groups_before(g))
                s, a = n % RING, group_bank(g)
                for k in range(k0, k1):
                    if rhs_ready:
                        rhs_ready(k)
                    nc.tensor.matmul(a[:, :], w_hi[:, s, k, :], rhs_hi(k), start=first and k == 0, stop=False)
                    nc.tensor.matmul(a[:, :], w_hi[:, s, k, :], rhs_lo(k), start=False, stop=False)
                    mm = nc.tensor.matmul(a[:, :], w_lo[:, s, k, :], rhs_hi(k), start=False,
                                          stop=last and k == KT - 1)
                return mm

            def finish(mm):
                mm.then_inc(used, 1)

            def of(t):
                return lambda k: t[:, k, :]

            def stat(norm, k):
                pe.wait_ge(sq_done, norm * KT + k + 1)
                nc.tensor.matmul(mix[norm % 2][:, :], ones[:, :], tmp[:, k % 2, :], start=(k == 0),
                                 stop=(k == KT - 1)).then_inc(stat_done, 1)

            def post_stat(norm):
                pe.wait_ge(ssq_done, (norm // 2 + 1) * (KT - 2))
                nc.tensor.matmul(mix[norm % 2][:, :], ones[:, :], rstd[:, :], start=True,
                                 stop=False).then_inc(stat_done, 1)
                pe.wait_ge(sq_done, (norm + 1) * KT)
                nc.tensor.matmul(mix[norm % 2][:, :], ones[:, :], tmp[:, (KT - 1) % 2, :], start=False,
                                 stop=True).then_inc(stat_done, 1)

            pe.wait_ge(ident_done, 1)
            pe.wait_ge(x_landed, 16 * NB)
            for k in range(KT):
                if k >= 2:
                    pe.wait_ge(x_done, k - 1)
                for b in range(NB):
                    mm = nc.tensor.transpose(trans[k % 2][:, b * P:(b + 1) * P], x_in[:, b, k * P:(k + 1) * P],
                                             ident[:, :])
                mm.then_inc(xt_ready, 1)
                if k >= 1:
                    stat(0, k - 1)
            stat(0, KT - 1)

            pe.wait_ge(const_done, 1)
            nc.tensor.transpose(mix[1][:, 0:1], freq_row[0:1, :], ident[0:1, 0:1]).then_inc(freq_t, 1)

            def first_two(n, g, norm):
                for k in range(KT):
                    stat(norm, k)
                    pe.wait_ge(h_done, norm // 2 * KT + k + 1)
                    for i in range(2):
                        if k == 0:
                            pe.wait_ge(wlo_done, n + i + 1)
                        mm = project(n + i, g + i, of(h_hi), of(h_lo), k, k + 1, starts=False)
                        if k == KT - 1:
                            finish(mm)

            def h_ready(k):
                pe.wait_ge(h_done, k + 1)

            finish(project(W_FOX, G_FOX, of(h_hi), of(h_lo), rhs_ready=h_ready))

            def fox_proj(pair, k0, k1):
                if pair == PAIRS:
                    return
                while k0 < k1:
                    j, a = divmod(k0, KT)
                    b = min(KT, a + k1 - k0)
                    mm = project(W_FOX + 1 + 3 * pair + j, G_FOX + 1 + 3 * pair + j, of(h_hi), of(h_lo), a, b)
                    if b == KT:
                        finish(mm)
                    k0 += b - a

            def fox_logits(hd, qb):
                p, side = divmod(hd, 2)
                j = hd * NB + qb
                if side == 0 and qb == 0:
                    pe.wait_ge(acc_free, G_FOX + 3 * p + 3)
                    pe.wait_ge(aug_landed[p % 2], 128 * (p // 2 + 1))
                if j == 0:
                    pe.wait_ge(mask_done, 1)
                if j >= 2:
                    pe.wait_ge(exp_done, j - 1)
                q1, q2, k1, k2 = fox_ops(p, side)
                n, qs = (qb + 1) * P, slice(qb * P, (qb + 1) * P)
                s = logit[j % 2]
                nc.tensor.matmul(s[:, 0:n], q1[:, qs], k1[:, 0:n], start=True, stop=False)
                nc.tensor.matmul(s[:, 0:n], q2[:, qs], k2[:, 0:n], start=False, stop=False)
                nc.tensor.matmul(s[:, qs], ident_r[:, :], masks[:, 0, P:2 * P], start=False,
                                 stop=True).then_inc(s_ready, 1)

            def fox_transposes(hd, i):
                j = fox_t(hd, i)
                if i == 0:
                    pe.wait_ge(prob_done, hd + 1)
                pe.wait_ge(t_free, j - 1) if j >= 2 else None
                at = 0
                for kb in ((0,), (1,), (2, 3))[i]:
                    for qb in range(kb, NB):
                        c = FOX_OFF[qb] + kb * P
                        mm = nc.tensor.transpose(trans[j % 2][:, at:at + P], prob[hd % 2][:, c:c + P], ident[:, :])
                        at += P
                mm.then_inc(t_ready, 1)

            def value_transposes(j, ready, count):
                pe.wait_ge(ready, count)
                if j >= 2:
                    pe.wait_ge(t_free, j - 1)
                for b in range(NB):
                    mm = nc.tensor.transpose(trans[j % 2][:, b * P:(b + 1) * P], tmp[:, 0, b * P:(b + 1) * P],
                                             ident[:, :])
                mm.then_inc(t_ready, 1)

            def fox_mix(hd):
                p = hd // 2
                pe.wait_ge(t_free, fox_t(hd, 2) + 1)
                if hd >= 2:
                    pe.wait_ge(o_done, hd - 1)
                o = mix[hd % 2]
                for kb in range(NB):
                    n = (NB - kb) * P
                    pt = slice(FOX_PT[kb], FOX_PT[kb] + n)
                    for v, t in ((v_hi, pt_hi), (v_hi, pt_lo), (v_lo, pt_hi)):
                        mm = nc.tensor.matmul(o[:, kb * P:SEQ], v[:, p % 2, kb, :], t[:, pt],
                                              start=(kb == 0 and v is v_hi and t is pt_hi),
                                              stop=(kb == NB - 1 and v is v_lo))
                mm.then_inc(pv_done, 1)

            def steps(at, n):
                end = min(at + n, 3 * KT * PAIRS)
                while at < end:
                    pair, k0 = divmod(at, 3 * KT)
                    k1 = min(3 * KT, k0 + end - at)
                    fox_proj(pair, k0, k1)
                    at += k1 - k0

            def early_out(w0, g0, heads0, k, o):
                pe.wait_ge(o_done, heads0 + 2 * k + 2)
                project(w0 + o, g0 + o, of(o_hi), of(o_lo), k, k + 1)

            steps(0, 3 * KT)
            fox_logits(0, 0)
            fox_logits(0, 1)
            steps(3 * KT, 4)
            fox_logits(0, 2)
            steps(3 * KT + 4, 4)
            fox_logits(0, 3)
            for h in range(HEADS):
                nxt = h + 1 < HEADS
                at = 4 * KT + 12 * h
                out_steps = h >= HEADS - 2
                k_out = 3 * (h - HEADS + 2)

                def early(k):
                    if out_steps:
                        for o in range(2):
                            early_out(W_FOX_OUT, G_FOX_OUT, 0, k, o)

                steps(at, 2)
                if h % 2 == 0:
                    value_transposes(fox_t(h, 0) - 1, acc_free, G_FOX + 4 + 3 * (h // 2))
                if h >= 1:
                    fox_mix(h - 1)
                if nxt:
                    fox_logits(h + 1, 0)
                steps(at + 2, 3)
                early(k_out)
                fox_transposes(h, 0)
                if nxt:
                    fox_logits(h + 1, 1)
                steps(at + 5, 3)
                early(k_out + 1)
                fox_transposes(h, 1)
                if nxt:
                    fox_logits(h + 1, 2)
                steps(at + 8, 2)
                early(k_out + 2)
                fox_transposes(h, 2)
                if nxt:
                    fox_logits(h + 1, 3)
                steps(at + 10, 2)
            fox_mix(HEADS - 1)

            def out_proj(w0, g0, norm, heads0):
                for o in range(KT):
                    finish(project(w0 + o, g0 + o, of(o_hi), of(o_lo), EARLY if o < 2 else 0, KT, rhs_ready=(
                        lambda k: pe.wait_ge(o_done, heads0 + 2 * k + 2)) if o == 0 else None))
                post_stat(norm)

            def mlp(layer, norm):
                n, g = W_MLP[layer] + 2, G_MLP[layer] + 2
                first_two(n - 2, g - 2, norm)
                for c in range(CHUNKS):
                    for j in range(2 if c == 0 else 0, F_CHUNK):
                        finish(project(n, g, of(h_hi), of(h_lo)))
                        n, g = n + 1, g + 1
                    done = (layer * CHUNKS + c) * F_CHUNK
                    for o in range(KT):
                        for hf in range(HALVES):
                            def u(t):
                                return lambda k: t[:, hf * KT + k, :]

                            def u_ready(k):
                                pe.wait_ge(u_done, done + hf * KT + k + 1)
                            finish(project(n, g, u(u_hi), u(u_lo), first=hf == 0, last=hf == HALVES - 1,
                                           rhs_ready=u_ready if o == 0 else None))
                            n += 1
                        g += 1
                post_stat(norm + 1)

            out_proj(W_FOX_OUT, G_FOX_OUT, 1, 0)
            mlp(0, 2)

            first_two(W_SWA, G_SWA, 4)

            def swa_proj(pair, k0, k1):
                if pair >= PAIRS:
                    return
                mm = project(W_SWA + 2 + pair, G_SWA + 2 + pair, of(h_hi), of(h_lo), k0, k1)
                if k1 == KT:
                    finish(mm)

            def swa_logits(hd, i):
                p, side = divmod(hd, 2)
                j = FOX_S + hd * 2 + i
                if side == 0 and i == 0:
                    pe.wait_ge(q_done, p + 2)
                    pe.wait_ge(q_copied[p % 2], 32 * (p // 2 + 1))
                    if p == 0:
                        pe.wait_ge(aug_set, 1)
                pe.wait_ge(exp_done, j - 1)
                q1, q2 = swa_q(p, side)
                k1, k2 = swa_k(hd // GROUP, side)
                s = logit[j % 2]
                nc.tensor.matmul(s[:, :], ident_r[:, :], masks[:, i, :], start=True, stop=False)
                for e in range(2):
                    qb = 2 * i + e
                    k0 = max(qb - 1, 0) * P
                    to = s[:, e * 2 * P + (P if qb == 0 else 0):(e + 1) * 2 * P]
                    qs, ks = slice(qb * P, (qb + 1) * P), slice(k0, (qb + 1) * P)
                    nc.tensor.matmul(to, q1[:, qs], k1[:, ks], start=False, stop=False)
                    mm = nc.tensor.matmul(to, q2[:, qs], k2[:, ks], start=False, stop=e == 1)
                mm.then_inc(s_ready, 1)

            def swa_t(hd, i):
                return SWA_T0 + 2 * hd + i

            def swa_transposes(hd, i):
                j = swa_t(hd, i)
                if i == 0:
                    pe.wait_ge(prob_done, HEADS + hd + 1)
                pe.wait_ge(t_free, j - 1)
                for e in range(2):
                    kb = 2 * i + e
                    for own, qb in ((1, kb), (0, kb + 1)):
                        if qb < NB:
                            c = qb * 2 * P + own * P
                            at = e * 2 * P + (1 - own) * P
                            mm = nc.tensor.transpose(trans[j % 2][:, at:at + P], prob[hd % 2][:, c:c + P], ident[:, :])
                mm.then_inc(t_ready, 1)

            def swa_mix(hd):
                pe.wait_ge(t_free, swa_t(hd, 1) + 1)
                pe.wait_ge(o_done, HEADS + hd - 1)
                o = mix[hd % 2]
                for kb in range(NB):
                    n = P * min(2, NB - kb)
                    for v, t in ((v_hi, pt_hi), (v_hi, pt_lo), (v_lo, pt_hi)):
                        mm = nc.tensor.matmul(o[:, kb * P:kb * P + n], v[:, 0, kb, :], t[:, kb * 2 * P:kb * 2 * P + n],
                                              start=(kb == 0 and v is v_hi and t is pt_hi), skip_group_check=True,
                                              stop=(kb == NB - 1 and v is v_lo))
                mm.then_inc(pv_done, 1)

            swa_proj(0, 0, KT)
            value_transposes(FOX_T, v_scaled, 1)
            swa_proj(1, 0, KT)
            swa_proj(2, 0, 4)
            swa_logits(0, 0)
            swa_logits(0, 1)
            swa_proj(2, 4, KT)
            for h in range(HEADS):
                pair, k0 = h // 2 + 3, h % 2 * 4
                nxt = h + 1 < HEADS
                out_steps = h >= HEADS - 2
                k_out = 3 * (h - HEADS + 2)

                def swa_early(k):
                    if out_steps:
                        for o in range(2):
                            early_out(W_SWA_OUT, G_SWA_OUT, HEADS, k, o)

                swa_proj(pair, k0, k0 + 1)
                if nxt:
                    swa_logits(h + 1, 0)
                swa_proj(pair, k0 + 1, k0 + 2)
                if h >= 1:
                    swa_mix(h - 1)
                if nxt:
                    swa_logits(h + 1, 1)
                swa_early(k_out)
                swa_transposes(h, 0)
                swa_proj(pair, k0 + 2, k0 + 3)
                swa_early(k_out + 1)
                swa_transposes(h, 1)
                swa_proj(pair, k0 + 3, k0 + 4)
                swa_early(k_out + 2)
            swa_mix(HEADS - 1)

            out_proj(W_SWA_OUT, G_SWA_OUT, 5, HEADS)
            mlp(1, 6)

            for k in range(KT):
                pe.wait_ge(x_done, KT * 4 + k + 1)
                if k >= 2:
                    pe.wait_ge(fin_done, k - 1)
                for b in range(NB):
                    mm = nc.tensor.transpose(trans[k % 2][:, b * P:(b + 1) * P], xT[:, k, b * P:(b + 1) * P],
                                             ident[:, :])
                mm.then_inc(fin_ready, 1)

        @block.scalar
        def _(sc):
            def split(n):
                if n >= W_END:
                    return
                sc.wait_ge(raw_landed[n % RAW], 16 * (n // RAW + 1))
                if n >= RING:
                    sc.wait_ge(used, n - RING + 1)
                nc.scalar.activation(w_hi[:, n % RING, :, :], w_raw[:, n % RAW, :, :], ACT.Copy).then_inc(whi_done, 1)

            def squares(norm, k, src, ready, count):
                sc.wait_ge(ready, count)
                to = tmp[:, k % 2, :]
                if norm % 2:
                    if k == 0:
                        to = rstd[:, :]
                    elif k >= 3:
                        sc.wait_ge(ssq_done, norm // 2 * (KT - 2) + k - 2)
                elif k >= 2:
                    sc.wait_ge(stat_done, stats_before(norm) + k - 1)
                nc.scalar.activation(to, src, ACT.Square).then_inc(sq_done, 1)

            def root(norm):
                sc.wait_ge(stat_done, stats_before(norm + 1))
                if norm == 0:
                    sc.wait_ge(eps_set, 1)
                nc.scalar.activation(tmp[:, 3, :], mix[norm % 2][:, :], ACT.Ln, scale=1.0 / D,
                                     bias=eps[:, 0:1]).then_inc(r0_step, 1)
                sc.wait_ge(r0_step, 2 * norm + 1)
                nc.scalar.activation(tmp[:, 3, :], tmp[:, 3, :], ACT.Exp, scale=-0.5).then_inc(r0_step, 1)

            def pre_tiles(kind, layer, norm, n):
                i = norm // 2
                for k in range(KT):
                    sc.wait_ge(x_done, i * KT + k + 1)
                    nc.scalar.activation(h_hi[:, k, :], xT[:, k, :], ACT.Copy,
                                         scale=gains[:, kind, layer, k:k + 1]).then_inc(hh_done, 1)
                    squares(norm, k, xT[:, k, :], x_done, i * KT + k + 1)
                root(norm)
                split(n)

            def pre_high(i):
                for k in range(KT):
                    sc.wait_ge(hf_done, i * KT + k + 1)
                    nc.scalar.activation(h_hi[:, k, :], tmp[:, k % 2, :], ACT.Copy).then_inc(hh_done, 1)

            nc.scalar.preload_act_table_set("natural_log_exp_and_others")
            with nc.allow_non_contiguous_dma(reason="small vectors, feature-major"):
                for i, g in enumerate((norm_pre_mix, norm_post_mix, norm_pre_ffn, norm_post_ffn)):
                    for layer in range(2):
                        sc.dma_start(gains[:, i, layer, :],
                                     g[layer].rearrange("(k p) -> p k", p=P)).then_inc(small_landed, 16)
                sc.wait_ge(ident_done, 1)
                sc.dma_start(b_f[P - HEADS:P, :], fox_b_f.rearrange("a h -> h a")).then_inc(small_landed, 16)
            sc.dma_start(sinks[:, :], swa_sinks.broadcast_to([P, HEADS])).then_inc(small_landed, 16)
            for n in range(AHEAD):
                split(n)
            for k in range(KT):
                if k == KT - 2:
                    sc.wait_ge(const_done, 1)
                    nc.scalar.activation(ident_r[:, :], ident[:, :], ACT.Copy)
                    nc.scalar.activation(masks[:, :, :], mask_src, ACT.Copy).then_inc(mask_done, 1)
                squares(0, k, xT[:, k, :], x_done, k + 1)
            root(0)
            pre_high(0)

            split(W_FOX + AHEAD)
            gate_rows = slice(P - 32, P)
            sc.wait_ge(gate_step, 1)
            nc.scalar.activation(tmp[gate_rows, 3, :], tmp[gate_rows, 3, :], ACT.Exp).then_inc(gate_act, 1)
            sc.wait_ge(gate_step, 2)
            nc.scalar.activation(tmp[gate_rows, 0, :], tmp[gate_rows, 0, :], ACT.Ln).then_inc(gate_act, 1)

            def fox_exp(hd, qb):
                j, n = hd * NB + qb, (qb + 1) * P
                sc.wait_ge(max_done, j + 1)
                if hd >= 2 and qb == 0:
                    sc.wait_ge(t_ready, fox_t(hd - 2, 2) + 1)
                nc.scalar.activation(prob[hd % 2][:, FOX_OFF[qb]:FOX_OFF[qb] + n], logit[j % 2][:, 0:n], ACT.Exp,
                                     bias=nmax[:, hd % 2, qb:qb + 1],
                                     accum_out=rsum[:, hd % 2, qb:qb + 1]).then_inc(exp_done, 1)

            def fox_high_q(p):
                sc.wait_ge(used, W_FOX + 2 + 3 * p)
                for side in range(2):
                    h = half(side)
                    last = nc.scalar.activation(fox_ops(p, side)[0][h, :], acc[(G_FOX + 1 + 3 * p) % 2][h, :],
                                                ACT.Copy, scale=SCALE)
                last.then_inc(hi_done, 1)

            def fox_high_k(p):
                sc.wait_ge(used, W_FOX + 3 + 3 * p)
                for side in range(2):
                    h = half(side)
                    last = nc.scalar.activation(fox_ops(p, side)[2][h, :], acc[(G_FOX + 2 + 3 * p) % 2][h, :],
                                                ACT.Copy)
                last.then_inc(hi_done, 1)

            def high_v(j, slot):
                sc.wait_ge(t_ready, j + 1)
                nc.scalar.activation(v_hi[:, slot, :, :].rearrange("p b n -> p (b n)"), trans[j % 2][:, :],
                                     ACT.Copy).then_inc(vh_done, 1)

            def high_t(j, at, n, free):
                sc.wait_ge(t_ready, j + 1)
                if free:
                    sc.wait_ge(pv_done, free)
                nc.scalar.activation(pt_hi[:, at:at + n], trans[j % 2][:, 0:n], ACT.Copy).then_inc(th_done, 1)

            def fox_high_t(hd, i):
                high_t(fox_t(hd, i), FOX_PT[i], (512, 384, 384)[i], hd)

            def high_o(hd, rows):
                p, side = divmod(hd % HEADS, 2)
                sc.wait_ge(pv_done, hd + 1)
                nc.scalar.activation(o_hi[half(side), p, :], mix[hd % 2][rows, :], ACT.Copy).then_inc(oh_done, 1)

            split(W_FOX + RING)
            fox_high_q(0)
            split(W_FOX + 1 + RING)
            fox_high_k(0)
            split(W_FOX + 2 + RING)
            for qb in range(NB):
                fox_exp(0, qb)
            split(W_FOX + 3 + RING)
            for h in range(HEADS):
                even, p = h % 2 == 0, h // 2
                nxt, proj = h + 1 < HEADS, p + 1 < PAIRS
                t = W_FOX + 1 + 3 * (p + 1)
                if even and proj:
                    fox_high_q(p + 1)
                if even:
                    high_v(7 * p, p % 2)
                if h >= 1:
                    high_o(h - 1, half((h - 1) % 2))
                if nxt:
                    fox_exp(h + 1, 0)
                if not even and proj:
                    split(t + 1 + RING)
                fox_high_t(h, 0)
                if nxt:
                    fox_exp(h + 1, 1)
                if even and proj:
                    split(t + RING)
                if not even and p + 2 < PAIRS:
                    split(t + 2 + RING)
                fox_high_t(h, 1)
                if nxt:
                    fox_exp(h + 1, 2)
                if even and proj:
                    fox_high_k(p + 1)
                fox_high_t(h, 2)
                if nxt:
                    fox_exp(h + 1, 3)
                if h == TABLE_SLOT:
                    sc.wait_ge(angle_done, 1)
                    nc.scalar.activation(sin_t[:, :], rope[1], ACT.Sin, scale=sign[:, 0:1])
                    nc.scalar.activation(cos_t[:, :], rope[2], ACT.Sin).then_inc(table_done, 1)
                    nc.scalar.preload_act_table_set("natural_log_exp_and_others")
            high_o(HEADS - 1, half(1))

            def out_proj(layer, w0, g0, norm):
                for o in range(KT):
                    split(w0 + o + AHEAD)
                    squares(norm, o, yT[:, o, :], acc_free, g0 + o + 1)
                root(norm)
                pre_tiles(2, layer, norm + 1, w0 + KT + AHEAD)

            def mlp(layer, norm):
                n, g = W_MLP[layer], G_MLP[layer]
                for c in range(CHUNKS):
                    for j in range(F_CHUNK):
                        if n > W_MLP[layer]:
                            split(n + AHEAD)
                        i = (layer * CHUNKS + c) * F_CHUNK + j
                        sc.wait_ge(acc_free, g + 1)
                        nc.scalar.activation(u_hi[:, j, :], tmp[:, j % 2, :], ACT.Square).then_inc(uhi_done, 1)
                        if j >= 2:
                            sc.wait_ge(u_done, i - 1)
                        nc.scalar.activation(tmp[:, 2 + j % 2, :], tmp[:, j % 2, :], ACT.Square).then_inc(squared, 1)
                        n, g = n + 1, g + 1
                    for o in range(KT):
                        for hf in range(HALVES):
                            split(n + AHEAD)
                            n += 1
                        g += 1
                        if c == CHUNKS - 1:
                            squares(norm + 1, o, yT[:, o, :], acc_free, g)
                root(norm + 1)

            out_proj(0, W_FOX_OUT, G_FOX_OUT, 1)
            mlp(0, 2)
            pre_tiles(0, 1, 4, W_SWA + AHEAD)

            def unrotated_copy(g, i):
                sc.wait_ge(used, g + 1 + W_SWA - G_SWA)
                if i >= 2:
                    sc.wait_ge(swap_landed[i % 2], 64 * (i // 2))
                elif i == 1:
                    sc.wait_ge(rstd_done, 5)
                nc.scalar.activation(unrotated[i % 2], acc[g % 2][:, :], ACT.Copy).then_inc(rot_done, 1)

            def swa_high_k():
                sc.wait_ge(rope_done, 1)
                for kv in range(2):
                    k1 = swa_k(kv, 0)[0]
                    for to in range(2):
                        last = nc.scalar.activation(k1[half(to), :], rope[2][half(kv), :], ACT.Copy)
                last.then_inc(hi_done, 1)

            def swa_high_q(p):
                sc.wait_ge(rope_done, 2 + p)
                nc.scalar.activation(swa_q(p, 0)[1], rope[2], ACT.Copy, scale=SCALE).then_inc(hi_done, 1)

            def swa_exp(hd, i):
                j = FOX_S + hd * 2 + i
                sc.wait_ge(max_done, j + 1)
                if i == 0:
                    if hd >= 2:
                        sc.wait_ge(t_ready, SWA_T0 + 2 * (hd - 2) + 2)
                for e in range(2):
                    qb = 2 * i + e
                    last = nc.scalar.activation(prob[hd % 2][:, qb * 2 * P:(qb + 1) * 2 * P],
                                                logit[j % 2][:, e * 2 * P:(e + 1) * 2 * P], ACT.Exp,
                                                bias=nmax[:, hd % 2, qb:qb + 1],
                                                accum_out=rsum[:, hd % 2, qb:qb + 1])
                last.then_inc(exp_done, 1)
                if i == 1:
                    nc.scalar.activation(esink[:, hd % 2, :], nmax[:, hd % 2, :], ACT.Exp,
                                         bias=sinks[:, hd:hd + 1]).then_inc(es_done, 1)

            def swa_high_t(hd, i):
                high_t(SWA_T0 + 2 * hd + i, i * 512, (512, 384)[i], HEADS + hd)

            unrotated_copy(G_SWA + 1, 0)
            split(W_SWA + RING)
            split(W_SWA + 1 + RING)
            unrotated_copy(G_SWA + 2, 1)
            swa_high_k()
            high_v(FOX_T, 0)
            split(W_SWA + 2 + RING)
            swa_high_q(0)
            unrotated_copy(G_SWA + 3, 2)
            split(W_SWA + 3 + RING)
            swa_exp(0, 0)
            swa_exp(0, 1)
            swa_high_q(1)
            for h in range(HEADS):
                even, p = h % 2 == 0, h // 2
                nxt, rotates = h + 1 < HEADS, p + 2 < PAIRS
                if even and rotates:
                    unrotated_copy(G_SWA + 2 + p + 2, 3 + p)
                if nxt:
                    swa_exp(h + 1, 0)
                if not even and p + 3 < PAIRS:
                    split(W_SWA + 4 + p + RING)
                if h >= 1:
                    high_o(HEADS + h - 1, half((h - 1) // GROUP))
                swa_high_t(h, 0)
                if nxt:
                    swa_exp(h + 1, 1)
                swa_high_t(h, 1)
                if not even and rotates:
                    swa_high_q(p + 2)
            high_o(2 * HEADS - 1, half(1))

            out_proj(1, W_SWA_OUT, G_SWA_OUT, 5)
            mlp(1, 6)
            for k in range(KT):
                sc.wait_ge(fin_ready, k + 1)
                nc.scalar.activation(yT[:, k, :], trans[k % 2][:, :], ACT.Copy).then_inc(fin_done, 1)

        @block.vector
        def _(ve):
            steps = [0]

            def own(ins):
                steps[0] += 1
                ins.then_inc(dve_step, 1)
                ve.wait_ge(dve_step, steps[0])

            f32 = lambda ap: ap.bitcast(F32)

            def split(n):
                if n >= W_END:
                    return
                ve.wait_ge(whi_done, n + 1)
                nc.vector.tensor_tensor(w_lo[:, n % RING, :, :], w_raw[:, n % RAW, :, :],
                                        f32(w_hi[:, n % RING, :, :]), ALU.subtract).then_inc(wlo_done, 1)

            def root(norm, n=None):
                ve.wait_ge(r0_step, 2 * norm + 1)
                own(nc.vector.tensor_scalar(tmp[:, 2, :], mix[norm % 2][:, :], -0.5 / D, -0.5 * EPS, ALU.mult, ALU.add))
                if n is not None:
                    split(n)
                ve.wait_ge(r0_step, 2 * norm + 2)
                own(nc.vector.tensor_tensor(tmp[:, 2, :], tmp[:, 2, :], tmp[:, 3, :], ALU.mult))
                own(nc.vector.tensor_tensor(tmp[:, 2, :], tmp[:, 2, :], tmp[:, 3, :], ALU.mult))
                nc.vector.scalar_tensor_tensor(rstd[:, :], tmp[:, 2, :], 1.5, tmp[:, 3, :], ALU.add,
                                               ALU.mult).then_inc(rstd_done, 1)
                ve.wait_ge(rstd_done, norm + 1)

            def add_squares(norm, k):
                if 1 <= k <= KT - 2:
                    if k >= 2:
                        ve.wait_ge(ssq_done, norm // 2 * (KT - 2) + k - 1)
                    ve.wait_ge(sq_done, norm * KT + k + 1)
                    nc.vector.tensor_tensor(rstd[:, :], rstd[:, :], tmp[:, k % 2, :], ALU.add).then_inc(ssq_done, 1)

            def scaled_y(kind, layer, k, before):
                if k >= 2:
                    ve.wait_ge(x_done, before + k - 1)
                nc.vector.scalar_tensor_tensor(tmp[:, 2 + k % 2, :], yT[:, k, :], gains[:, kind, layer, k:k + 1],
                                               rstd[:, :], ALU.mult, ALU.mult).then_inc(yn_done, 1)

            def add_y(k, count):
                ve.wait_ge(yn_done, count)
                nc.vector.tensor_tensor(xT[:, k, :], xT[:, k, :], tmp[:, 2 + k % 2, :], ALU.add).then_inc(x_done, 1)

            def post_pre(kind, layer, norm, kind2, layer2):
                root(norm)
                base, before = (norm + 1) // 2 * KT, norm // 2 * KT

                def low(k):
                    if kind2 >= 0:
                        ve.wait_ge(hh_done, base + k + 1)
                        nc.vector.scalar_tensor_tensor(h_lo[:, k, :], xT[:, k, :], gains[:, kind2, layer2, k:k + 1],
                                                       f32(h_hi[:, k, :]), ALU.mult, ALU.subtract).then_inc(h_done, 1)

                scaled_y(kind, layer, 0, base)
                for k in range(KT):
                    if k + 1 < KT:
                        scaled_y(kind, layer, k + 1, base)
                    add_y(k, before + k + 1)
                    if k >= 1:
                        low(k - 1)
                low(KT - 1)
            def pre(kind, layer, norm):
                root(norm)
                base = norm // 2 * KT

                def low(k):
                    ve.wait_ge(hh_done, base + k + 1)
                    nc.vector.tensor_tensor(h_lo[:, k, :], tmp[:, k % 2, :], f32(h_hi[:, k, :]),
                                            ALU.subtract).then_inc(h_done, 1)
                for k in range(KT):
                    if k >= 2:
                        low(k - 2)
                        ve.wait_ge(h_done, base + k - 1)
                    nc.vector.scalar_tensor_tensor(tmp[:, k % 2, :], xT[:, k, :], gains[:, kind, layer, k:k + 1],
                                                   rstd[:, :], ALU.mult, ALU.mult).then_inc(hf_done, 1)
                low(KT - 2)
                low(KT - 1)

            def gates():
                r = slice(P - 32, P)
                z, e, u, c = (tmp[r, i, :] for i in (1, 3, 0, 2))
                ve.wait_ge(used, W_FOX + 1)
                nc.vector.tensor_scalar(z, acc[G_FOX % 2][r, :], b_f[r, 0:1], None, ALU.add).then_inc(acc_free, 1)
                ve.wait_ge(acc_free, G_FOX + 1)
                nc.vector.scalar_tensor_tensor(e, z, -1.0, z, ALU.mult, ALU.min).then_inc(gate_step, 1)
                ve.wait_ge(gate_act, 1)
                own(nc.vector.tensor_scalar(u, e, 1.0, None, ALU.add))
                own(nc.vector.scalar_tensor_tensor(e, u, -1.0, e, ALU.add, ALU.subtract))
                nc.vector.memset(c, 0.0).then_inc(gate_step, 1)
                ve.wait_ge(gate_act, 2)
                own(nc.vector.tensor_tensor(u, u, e, ALU.subtract))
                own(nc.vector.scalar_tensor_tensor(z, z, 0.0, u, ALU.min, ALU.subtract))
                own(nc.vector.tensor_tensor_scan(e, z, c, 0.0, ALU.add, ALU.add))
                own(nc.vector.tensor_copy(pt_hi[r, 0:SEQ], e))
                nc.vector.tensor_tensor(pt_lo[r, 0:SEQ], e, f32(pt_hi[r, 0:SEQ]), ALU.subtract).then_inc(c_done, 1)

            def low_q(src, q1, high, end):
                for side in range(2):
                    last = nc.vector.scalar_tensor_tensor(q1[side][half(1 - side), :], src[half(side), :], SCALE,
                                                          f32(high[side][half(side), :]), ALU.mult, ALU.subtract)
                last.then_inc(end, 1)

            def fox_low_q(p):
                ve.wait_ge(hi_done, 2 * p + 1)
                q1 = [fox_ops(p, s)[0] for s in range(2)]
                low_q(acc[(G_FOX + 1 + 3 * p) % 2], q1, q1, acc_free)

            def fox_low_k(p):
                ve.wait_ge(hi_done, 2 * p + 2)
                for side in range(2):
                    _, _, k1, k2 = fox_ops(p, side)
                    h = half(side)
                    last = nc.vector.tensor_tensor(k2[h, :], acc[(G_FOX + 2 + 3 * p) % 2][h, :], f32(k1[h, :]),
                                                   ALU.subtract)
                last.then_inc(acc_free, 1)

            def value_copy(n, g):
                ve.wait_ge(used, n + 1)
                nc.vector.tensor_copy(tmp[:, 0, :], acc[g % 2][:, :]).then_inc(acc_free, 1)

            def low_v(j, slot, i):
                ve.wait_ge(vh_done, i + 1)
                nc.vector.tensor_tensor(v_lo[:, slot, :, :].rearrange("p b n -> p (b n)"), trans[j % 2][:, :],
                                        f32(v_hi[:, slot, :, :].rearrange("p b n -> p (b n)")),
                                        ALU.subtract).then_inc(t_free, 1)

            def low_t(i, j, at, n):
                ve.wait_ge(th_done, i + 1)
                nc.vector.tensor_tensor(pt_lo[:, at:at + n], trans[j % 2][:, 0:n], f32(pt_hi[:, at:at + n]),
                                        ALU.subtract).then_inc(t_free, 1)

            def fox_low_t(hd, i):
                low_t(3 * hd + i, fox_t(hd, i), FOX_PT[i], (512, 384, 384)[i])

            def swa_low_t(hd, i):
                low_t(3 * HEADS + 2 * hd + i, SWA_T0 + 2 * hd + i, i * 512, (512, 384)[i])

            def low_o(hd, rows):
                p, side = divmod(hd % HEADS, 2)
                ve.wait_ge(oh_done, hd + 1)
                nc.vector.tensor_tensor(o_lo[half(side), p, :], mix[hd % 2][rows, :], f32(o_hi[half(side), p, :]),
                                        ALU.subtract).then_inc(o_done, 1)

            def fox_max(hd, qb):
                j = hd * NB + qb
                ve.wait_ge(s_ready, j + 1)
                nc.vector.reduce_max(nmax[:, hd % 2, qb:qb + 1], logit[j % 2][:, 0:(qb + 1) * P], AX_X,
                                     negate=True).then_inc(max_done, 1)

            def fox_norm(hd):
                ve.wait_ge(exp_done, (hd + 1) * NB)
                own(nc.vector.reciprocal(rden[:, hd % 2, :], rsum[:, hd % 2, :]))
                for qb in range(NB):
                    pr = prob[hd % 2][:, FOX_OFF[qb]:FOX_OFF[qb] + (qb + 1) * P]
                    last = nc.vector.tensor_scalar(pr, pr, rden[:, hd % 2, qb:qb + 1], None, ALU.mult)
                last.then_inc(prob_done, 1)

            def swa_max(hd, i):
                j = FOX_S + hd * 2 + i
                ve.wait_ge(s_ready, j + 1)
                nm = nmax[:, hd % 2, 2 * i:2 * i + 2]
                own(nc.vector.reduce_max(nm, logit[j % 2][:, :].rearrange("p (e n) -> p e n", e=2), AX_X, negate=True))
                nc.vector.tensor_scalar(nm, nm, nsinks[:, hd:hd + 1], None, ALU.min).then_inc(max_done, 1)

            def swa_norm(hd):
                ve.wait_ge(es_done, hd + 1)
                own(nc.vector.tensor_tensor(rden[:, hd % 2, :], rsum[:, hd % 2, :], esink[:, hd % 2, :], ALU.add))
                own(nc.vector.reciprocal(rden[:, hd % 2, :], rden[:, hd % 2, :]))
                for qb in range(NB):
                    pr = prob[hd % 2][:, qb * 2 * P:(qb + 1) * 2 * P]
                    last = nc.vector.tensor_scalar(pr, pr, rden[:, hd % 2, qb:qb + 1], None, ALU.mult)
                last.then_inc(prob_done, 1)

            def rotate_cos(g, i):
                ve.wait_ge(rot_done, i + 1)
                nc.vector.tensor_tensor(rope[1], acc[g % 2][:, :], cos_t[:, :], ALU.mult).then_inc(acc_free, 1)

            def rotate_sin(i):
                ve.wait_ge(swap_landed[i % 2], 64 * (i // 2 + 1))
                own(nc.vector.tensor_tensor(swapped[i % 2], swapped[i % 2], sin_t[:, :], ALU.mult))
                nc.vector.tensor_tensor(rope[2], swapped[i % 2], rope[1], ALU.add).then_inc(rope_done, 1)

            def swa_low_k():
                ve.wait_ge(hi_done, 2 * PAIRS + 1)
                for kv in range(KV_HEADS):
                    for side in range(2):
                        k1, k2 = swa_k(kv, side)
                        last = nc.vector.tensor_tensor(k2[half(side), :], rope[2][half(kv), :], f32(k1[half(kv), :]),
                                                       ALU.subtract)
                last.then_inc(q_done, 1)

            def swa_low_q(p):
                ve.wait_ge(hi_done, 2 * PAIRS + 2 + p)
                low_q(rope[2], [swa_q(p, s)[0] for s in range(2)], [swa_q(p, s)[1] for s in range(2)], q_done)

            def out_proj(w0, g0, norm):
                for o in range(KT):
                    split(w0 + o + AHEAD)
                    ve.wait_ge(used, w0 + o + 1)
                    nc.vector.tensor_copy(yT[:, o, :], acc[(g0 + o) % 2][:, :]).then_inc(acc_free, 1)
                    add_squares(norm, o - 1)

            def mlp(layer, norm):
                n, g = W_MLP[layer], G_MLP[layer]
                for c in range(CHUNKS):
                    for j in range(F_CHUNK):
                        if n > W_MLP[layer]:
                            split(n + AHEAD)
                        i = (layer * CHUNKS + c) * F_CHUNK + j
                        ve.wait_ge(used, n + 1)
                        if j >= 2:
                            ve.wait_ge(squared, i - 1)
                        nc.vector.scalar_tensor_tensor(tmp[:, j % 2, :], group_bank(g)[:, :], 0.0, rstd[:, :],
                                                       ALU.max, ALU.mult).then_inc(acc_free, 1)
                        ve.wait_ge(squared, i + 1)
                        nc.vector.tensor_tensor(u_lo[:, j, :], tmp[:, 2 + j % 2, :], f32(u_hi[:, j, :]),
                                                ALU.subtract).then_inc(u_done, 1)
                        n, g = n + 1, g + 1
                    for o in range(KT):
                        for _ in range(HALVES):
                            split(n + AHEAD)
                            n += 1
                        ve.wait_ge(used, n)
                        if c == 0:
                            nc.vector.tensor_copy(yT[:, o, :], group_bank(g)[:, :]).then_inc(acc_free, 1)
                        else:
                            nc.vector.tensor_tensor(yT[:, o, :], group_bank(g)[:, :], yT[:, o, :],
                                                    ALU.add).then_inc(acc_free, 1)
                            add_squares(norm, o - 1)
                        g += 1

            def angles(part):
                turns, ang, quarter = rope[0], rope[1], rope[2]
                pieces = two_pi_parts()
                pi = 3.1415925
                if part == 0:
                    ve.wait_ge(pos_landed, 16)
                    ve.wait_ge(freq_t, 1)
                    own(nc.vector.tensor_copy(turns, rope[2].bitcast(I32)))
                    own(nc.vector.tensor_copy(freq[:, :], mix[1][:, 0:1]))
                elif part == 1:
                    own(nc.vector.tensor_scalar(ang, turns, freq[:, 0:1], None, ALU.mult))
                    magic = 1.5 * 2.0 ** 23
                    own(nc.vector.tensor_scalar(turns, ang, 0.5 / np.pi, magic, ALU.mult, ALU.add))
                    own(nc.vector.tensor_scalar(turns, turns, -magic, None, ALU.add))
                elif part < 5:
                    for piece in pieces[2 * (part - 2):2 * (part - 1)]:
                        own(nc.vector.scalar_tensor_tensor(ang, turns, -piece, ang, ALU.mult, ALU.add))
                elif part == 5:
                    own(nc.vector.tensor_scalar(ang, ang, pi, -pi, ALU.min, ALU.max))
                    own(nc.vector.tensor_scalar(quarter, ang, np.pi / 2, None, ALU.add))
                elif part == 6:
                    own(nc.vector.tensor_scalar(turns, quarter, pi, -2 * np.pi, ALU.is_gt, ALU.mult))
                    own(nc.vector.tensor_tensor(quarter, quarter, turns, ALU.add))
                    nc.vector.tensor_scalar(quarter, quarter, pi, -pi, ALU.min, ALU.max).then_inc(angle_done, 1)

            nc.vector.memset(eps[:, :], EPS).then_inc(eps_set, 1)
            for n in range(AHEAD):
                split(n)
            for k in range(KT):
                ve.wait_ge(xt_ready, k + 1)
                if k == KT - 2:
                    ve.wait_ge(mask_done, 1)
                nc.vector.tensor_copy(xT[:, k, :], trans[k % 2][:, :]).then_inc(x_done, 1)

            ve.wait_ge(small_landed, 16 * 10)
            own(nc.vector.tensor_scalar(nsinks[:, :], sinks[:, :], -1.0, None, ALU.mult))
            pre(0, 0, 0)

            split(W_FOX + AHEAD)
            gates()
            split(W_FOX + RING)
            fox_low_q(0)
            split(W_FOX + 1 + RING)
            fox_low_k(0)
            value_copy(W_FOX + 3, G_FOX + 3)
            split(W_FOX + 2 + RING)
            angles(0)
            for qb in range(NB):
                fox_max(0, qb)
            split(W_FOX + 3 + RING)
            fox_norm(0)
            for h in range(HEADS):
                even, p = h % 2 == 0, h // 2
                nxt, proj = h + 1 < HEADS, p + 1 < PAIRS
                t = W_FOX + 1 + 3 * (p + 1)
                if even and proj:
                    fox_low_q(p + 1)
                if even:
                    low_v(7 * p, p % 2, p)
                if nxt:
                    fox_max(h + 1, 0)
                if h >= 1:
                    low_o(h - 1, half((h - 1) % 2))
                if not even and proj:
                    value_copy(t + 2, G_FOX + 3 + 3 * (p + 1))
                    split(t + 1 + RING)
                if nxt:
                    fox_max(h + 1, 1)
                fox_low_t(h, 0)
                if even and proj:
                    split(t + RING)
                if not even and p + 2 < PAIRS:
                    split(t + 2 + RING)
                if nxt:
                    fox_max(h + 1, 2)
                fox_low_t(h, 1)
                if even and proj:
                    fox_low_k(p + 1)
                if nxt:
                    fox_max(h + 1, 3)
                fox_low_t(h, 2)
                if nxt:
                    fox_norm(h + 1)
                if not even:
                    angles(p + 1)
            low_o(HEADS - 1, half(1))

            out_proj(W_FOX_OUT, G_FOX_OUT, 1)
            post_pre(1, 0, 1, 2, 0)
            root(2, W_MLP[0] + AHEAD)
            mlp(0, 3)
            post_pre(3, 0, 3, 0, 1)

            ve.wait_ge(stat_done, stats_before(5))
            value_copy(W_SWA, G_SWA)
            root(4, W_SWA + AHEAD)
            ve.wait_ge(table_done, 1)
            own(nc.vector.tensor_tensor(cos_t[:, :], cos_t[:, :], rstd[:, :], ALU.mult))
            rotate_cos(G_SWA + 1, 0)
            nc.vector.tensor_tensor(tmp[:, 0, :], tmp[:, 0, :], rstd[:, :], ALU.mult).then_inc(v_scaled, 1)
            own(nc.vector.tensor_tensor(sin_t[:, :], sin_t[:, :], rstd[:, :], ALU.mult))
            split(W_SWA + RING)
            split(W_SWA + 1 + RING)
            rotate_sin(0)
            low_v(FOX_T, 0, PAIRS)
            swa_low_k()
            rotate_cos(G_SWA + 2, 1)
            split(W_SWA + 2 + RING)
            rotate_sin(1)
            swa_low_q(0)
            rotate_cos(G_SWA + 3, 2)
            split(W_SWA + 3 + RING)
            swa_max(0, 0)
            swa_max(0, 1)
            rotate_sin(2)
            swa_norm(0)
            swa_low_q(1)
            for h in range(HEADS):
                even, p = h % 2 == 0, h // 2
                nxt, rotates = h + 1 < HEADS, p + 2 < PAIRS
                if nxt:
                    swa_max(h + 1, 0)
                if even and 1 <= p < PAIRS - 1:
                    swa_low_q(p + 1)
                if even and rotates:
                    rotate_cos(G_SWA + 2 + p + 2, 3 + p)
                if not even and rotates:
                    rotate_sin(3 + p)
                if nxt:
                    swa_max(h + 1, 1)
                if h >= 1:
                    low_o(HEADS + h - 1, half((h - 1) // GROUP))
                swa_low_t(h, 0)
                swa_low_t(h, 1)
                if nxt:
                    swa_norm(h + 1)
                if not even and p + 3 < PAIRS:
                    split(W_SWA + 4 + p + RING)
            low_o(2 * HEADS - 1, half(1))

            out_proj(W_SWA_OUT, G_SWA_OUT, 5)
            post_pre(1, 1, 5, 2, 1)
            root(6, W_MLP[1] + AHEAD)
            mlp(1, 7)
            post_pre(3, 1, 7, -1, -1)


_INS = ["x", "positions", "fox_w_in", "fox_b_f", "fox_w_out", "swa_w_in", "swa_sinks", "swa_w_out",
        "norm_pre_mix", "norm_post_mix", "norm_pre_ffn", "norm_post_ffn", "mlp_w_up", "mlp_w_down"]


def kernel(**inputs):
    import numpy as _np
    import concourse.bacc as _bacc
    from concourse import mybir as _mybir
    from concourse.bass_utils import run_bass_kernel_spmd as _run

    nc = _bacc.Bacc("TRN2", target_bir_lowering=False, num_devices=1)
    arrays, args = {}, []
    for name in _INS:
        a = _np.ascontiguousarray(inputs[name])
        arrays[f"in_{name}_dram"] = a
        args.append(nc.dram_tensor(f"in_{name}_dram", a.shape, _mybir.dt.from_np(a.dtype), kind="ExternalInput").ap())
    args.append(nc.dram_tensor("out_0_dram", (1, SEQ, D), F32, kind="ExternalOutput").ap())
    trunk(nc, *args)
    r = _run(nc, [arrays], core_ids=[0])
    return r.results[0]["out_0_dram"]
```

```python
from contextlib import ExitStack

import numpy as np

import concourse.bass as bass
from concourse import mybir

F32 = mybir.dt.float32
F32R = mybir.dt.float32r
I32 = mybir.dt.int32
ALU = mybir.AluOpType
ACT = mybir.ActivationFunctionType
AX_X = mybir.AxisListType.X

P = 128
SEQ = 512
D = 1024
D_FF = 4096
HD = 64
HEADS = 16
KV_HEADS = 2
GROUP = HEADS // KV_HEADS
NB = SEQ // P
KT = D // P
PAIRS = HEADS // 2
QD = HEADS * HD
KVD = KV_HEADS * HD
FOX_IN = 3 * QD + HEADS
EPS = 1e-6
SCALE = HD ** -0.5
NEG = -1e30
ROPE_THETA = 10000.0

RING = 4
RAW = 2
MLP_AHEAD = 2
FIRST_SPLITS = (3, 6)
AHEAD = RING - 1

F_CHUNK = 16
CHUNKS = D_FF // P // F_CHUNK
HALVES = F_CHUNK // KT

W_FOX = 0
W_FOX_OUT = W_FOX + 1 + 3 * PAIRS
W_MLP = [W_FOX_OUT + KT, 0]
MLP_TILES = CHUNKS * (F_CHUNK + KT * HALVES)
W_SWA = W_MLP[0] + MLP_TILES
W_SWA_OUT = W_SWA + 2 + PAIRS
W_MLP[1] = W_SWA_OUT + KT
W_END = W_MLP[1] + MLP_TILES
G_FOX = 0
G_FOX_OUT = G_FOX + 1 + 3 * PAIRS
G_MLP = [G_FOX_OUT + KT, 0]
MLP_GROUPS = CHUNKS * (F_CHUNK + KT)
G_SWA = G_MLP[0] + MLP_GROUPS
G_SWA_OUT = G_SWA + 2 + PAIRS
G_MLP[1] = G_SWA_OUT + KT

EARLY = 6

TABLE_SLOT = HEADS - 3

FOX_OFF = [0, 128, 384, 768]
FOX_PT = [0, 512, 896, 1152]
FOX_P = 1280
SWA_P = NB * 2 * P
DIRECT = 2
DVE_SCALES = 1


def inv_freq():
    return np.float32(1) / (ROPE_THETA ** (np.arange(0, HD, 2) / HD)).astype(np.float32)


def two_pi_parts():
    rest, parts = 2 * np.pi, []
    for _ in range(5):
        step = 2.0 ** (np.floor(np.log2(rest)) - 5)
        parts.append(float(np.floor(rest / step) * step))
        rest -= parts[-1]
    return parts + [float(np.float32(rest))]


def trunk(nc, x, positions, fox_w_in, fox_b_f, fox_w_out, swa_w_in, swa_sinks, swa_w_out,
          norm_pre_mix, norm_post_mix, norm_pre_ffn, norm_post_ffn, mlp_w_up, mlp_w_down, out):
    with ExitStack() as ctx:
        def sb(name, shape, dt=F32):
            return ctx.enter_context(nc.sbuf_tensor(name, shape, dt))

        def sem(name):
            return ctx.enter_context(nc.semaphore(name))

        xT = sb("xT", [P, KT, SEQ])
        yT = sb("yT", [P, KT, SEQ])
        h_hi = sb("h_hi", [P, KT, SEQ], F32R)
        h_lo = sb("h_lo", [P, KT, SEQ], F32R)
        w_raw = sb("w_raw", [P, RAW, KT, P])
        w_hi = sb("w_hi", [P, RING, KT, P], F32R)
        w_lo = sb("w_lo", [P, RING, KT, P], F32R)
        act = sb("act", [P, 32, SEQ], F32R)
        pt_hi = sb("pt_hi", [P, FOX_P], F32R)
        pt_lo = sb("pt_lo", [P, FOX_P], F32R)
        v_hi = sb("v_hi", [P, 2, NB, P], F32R)
        v_lo = sb("v_lo", [P, 2, NB, P], F32R)
        tmp = sb("tmp", [P, 4, SEQ])
        rstd = sb("rstd", [P, SEQ])
        sq_sum = sb("sq_sum", [P, SEQ])
        cos_t = sb("cos_t", [P, SEQ])
        sin_t = sb("sin_t", [P, SEQ])
        ident = sb("ident", [P, P])
        ones = sb("ones", [P, P])
        ident_r = sb("ident_r", [P, P], F32R)
        masks = sb("masks", [P, 6 * P], F32R)
        gains = sb("gains", [P, 4, 2, KT])
        freq_row = sb("freq_row", [1, P])
        freq = sb("freq", [P, 1])
        sign = sb("sign", [P, 1])
        eps = sb("eps", [P, 1])
        b_f = sb("b_f", [P, 1])
        sinks = sb("sinks", [P, HEADS])
        nsinks = sb("nsinks", [P, HEADS])
        pool_flag = sb("pool_flag", [P, 1])
        nmax = sb("nmax", [P, 2, NB])
        rsum = sb("rsum", [P, 2, NB])
        esink = sb("esink", [P, 2, NB])
        rden = sb("rden", [P, 2, NB])

        o_hi, o_lo = act[:, 0:8, :], act[:, 8:16, :]
        u_hi, u_lo = act[:, 0:F_CHUNK, :], act[:, F_CHUNK:2 * F_CHUNK, :]
        y_flat = yT[:, :, :].rearrange("p k t -> p (k t)")
        prob = [y_flat[:, h * FOX_P:(h + 1) * FOX_P] for h in range(2)]
        swa_prob = [y_flat[:, h * SWA_P:(h + 1) * SWA_P] for h in range(2)]
        rope = [y_flat[:, (5 + i) * SEQ:(6 + i) * SEQ] for i in range(3)]
        unrotated = [tmp[:, 1, :], tmp[:, 2, :]]
        swapped = [rope[0], tmp[:, 3, :]]
        x_in = y_flat.rearrange("p (b d) -> p b d", b=NB)
        mask_src = xT[:, KT - 2:KT, :].rearrange("p k t -> p (k t)")[:, 0:6 * P]

        def fox_ops(p, side):
            s = 16 + 8 * (p % 2) + 4 * side
            return act[:, s, :], act[:, s + 1, :], act[:, s + 2, :], act[:, s + 3, :]

        def swa_q(p, side):
            s = 16 + 3 * (p % 2)
            return act[:, s + side, :], act[:, s + 2, :]

        def swa_q_low(p):
            return act[:, 22 + p % 2, :]

        k_rotated = y_flat[:, 2 * SWA_P:2 * SWA_P + SEQ]

        def swa_k(kv, side):
            return act[:, 24 + kv, :], act[:, 26 + 2 * kv + side, :]

        def fox_scaled(p):
            return (tmp[:, 1, :], tmp[:, 2, :]) if p else (y_flat[:, 0:SEQ], y_flat[:, SEQ:2 * SEQ])

        def half(side):
            return slice(HD * side, HD * side + HD)

        def bank(name):
            return ctx.enter_context(nc.psum_tensor(name, [P, SEQ], F32))

        acc = [bank(f"acc{i}") for i in range(2)]
        logit = [bank(f"logit{i}") for i in range(2)]
        mlp_acc = acc + logit
        trans = [bank(f"trans{i}") for i in range(2)]
        mix = [bank(f"mix{i}") for i in range(2)]

        out_banks = acc + logit + trans + mix
        x_banks = [mix[0], acc[0], acc[1], mix[1], logit[0], logit[1], trans[0], trans[1]]

        c_dram = nc.dram_tensor("c_scratch", (HEADS, 2, SEQ), F32R).ap()

        raw_landed = [sem(f"raw_landed{i}") for i in range(RAW)]
        whi_done = sem("whi_done")
        wlo_done = sem("wlo_done")
        used = sem("used")
        acc_free = sem("acc_free")
        x_landed = [sem(f"x_landed{b}") for b in range(NB)]
        gain0_landed = sem("gain0_landed")
        small_landed = sem("small_landed")
        pos_landed = sem("pos_landed")
        pool_step = sem("pool_step")
        ident_done = sem("ident_done")
        const_done = sem("const_done")
        mask_done = sem("mask_done")
        freq_t = sem("freq_t")
        angle_done = sem("angle_done")
        table_done = sem("table_done")
        xt_ready = sem("xt_ready")
        x_done = sem("x_done")
        sq_done = sem("sq_done")
        stat_done = sem("stat_done")
        xsq_done = sem("xsq_done")
        ssq_done = sem("ssq_done")
        eps_set = sem("eps_set")
        r0_step = sem("r0_step")
        rstd_done = sem("rstd_done")
        hh_done = sem("hh_done")
        h_done = sem("h_done")
        yn_done = sem("yn_done")
        dve_step = sem("dve_step")
        squared = sem("squared")
        uhi_done = sem("uhi_done")
        u_done = sem("u_done")
        gate_step = sem("gate_step")
        gate_act = sem("gate_act")
        c_done = sem("c_done")
        c_stored = sem("c_stored")
        aug_set = sem("aug_set")
        aug_landed = [sem(f"aug_landed{i}") for i in range(2)]
        swap_landed = [sem(f"swap_landed{i}") for i in range(2)]
        q_copied = [sem(f"q_copied{i}") for i in range(2)]
        qk_done = sem("qk_done")
        aug0_landed = [sem(f"aug0_landed{i}") for i in range(2)]
        q_done = sem("q_done")
        k_done = sem("k_done")
        rden_done = sem("rden_done")
        scaled = sem("scaled")
        hi_done = sem("hi_done")
        vh_done = sem("vh_done")
        s_ready = sem("s_ready")
        max_done = sem("max_done")
        exp_done = sem("exp_done")
        prob_done = sem("prob_done")
        t_ready = sem("t_ready")
        th_done = sem("th_done")
        t_free = sem("t_free")
        pv_done = sem("pv_done")
        oh_done = sem("oh_done")
        o_done = sem("o_done")
        rot_done = sem("rot_done")
        rope_done = sem("rope_done")
        v_scaled = sem("v_scaled")
        es_done = sem("es_done")
        fin_ready = sem("fin_ready")
        fin_done = sem("fin_done")
        stored = sem("stored")

        def group_bank(g):
            for base in G_MLP:
                if base <= g < base + MLP_GROUPS:
                    return mlp_acc[(g - base) % len(mlp_acc)]
            return acc[g % 2]

        def groups_before(g, looped):
            if looped:
                return g + 1 - len(mlp_acc)
            for base in G_MLP:
                if base <= g < base + MLP_GROUPS:
                    return max(base, g + 1 - len(mlp_acc))
            return g - 1

        def stats_before(norm):
            return KT + 2 * (norm - 1) if norm else 0

        block = ctx.enter_context(nc.Block())

        def fox_t(hd, i):
            return 7 * (hd // 2) + 1 + 3 * (hd % 2) + i

        FOX_S, FOX_T = HEADS * NB, PAIRS * 7
        SWA_T0 = FOX_T + 1

        @block.sync
        def _(sp):
            def load(n, src, r=0):
                if n >= RAW:
                    sp.wait_ge(wlo_done, n - RAW + 1 + r)
                sp.dma_start(w_raw[:, n % RAW, :, :],
                             src.rearrange("(k p) n -> p k n", p=P)).then_inc(raw_landed[n % RAW], 16)

            w_in = fox_w_in[0]
            load(W_FOX, w_in[:, FOX_IN - P:FOX_IN])
            xr = x.rearrange("a (b p) d -> p (a b) d", p=P)
            for b in range(NB):
                sp.dma_start(x_in[:, b, :], xr[:, b, :]).then_inc(x_landed[b], 16)
            for p in range(PAIRS):
                for j in range(3):
                    load(W_FOX + 1 + 3 * p + j, w_in[:, j * QD + p * P:j * QD + (p + 1) * P])
            for o in range(KT):
                load(W_FOX_OUT + o, fox_w_out[0][:, o * P:(o + 1) * P])

            def load_mlp(layer):
                n, up, down = W_MLP[layer], mlp_w_up[layer], mlp_w_down[layer]
                for c in range(CHUNKS):
                    with sp.Fori(0, F_CHUNK // RING) as it:
                        r = it * RING
                        for i in range(RING):
                            load(n + i, up[:, bass.ds((r + c * F_CHUNK + i) * P, P)], r)
                    n += F_CHUNK
                    with sp.Fori(0, KT * HALVES // RING) as it:
                        o = it * (RING // HALVES)
                        for i in range(RING // HALVES):
                            for hf in range(HALVES):
                                f = (c * F_CHUNK + hf * KT) * P
                                load(n + i * HALVES + hf, down[f:f + KT * P, bass.ds((o + i) * P, P)], o * HALVES)
                    n += KT * HALVES

            load_mlp(0)
            w_in2 = swa_w_in[0]
            load(W_SWA, w_in2[:, QD + KVD:QD + 2 * KVD])
            load(W_SWA + 1, w_in2[:, QD:QD + KVD])
            for p in range(PAIRS):
                load(W_SWA + 2 + p, w_in2[:, p * P:(p + 1) * P])
            for o in range(KT):
                load(W_SWA_OUT + o, swa_w_out[0][:, o * P:(o + 1) * P])
            load_mlp(1)

            outr = out.rearrange("a (b p) (k f) -> k p (a b) f", p=P, f=P)
            for k in range(KT):
                sp.wait_ge(fin_done, k + 1)
                sp.dma_start(outr[k], yT[:, k, :].rearrange("p (b f) -> p b f", b=NB)).then_inc(stored, 16)
            sp.wait_ge(stored, 16 * KT)

        @block.gpsimd
        def _(pool):
            step = [0]

            def done(ins):
                step[0] += 1
                ins.then_inc(pool_step, 1)
                pool.wait_ge(pool_step, step[0])

            done(nc.gpsimd.memset(ident[:, :], 0.0))
            done(nc.gpsimd.affine_select(out=ident[:, :], in_=ident[:, :], compare_op=ALU.not_equal, fill=1.0,
                                         base=0, pattern=[[-1, P]], channel_multiplier=1))
            done(nc.gpsimd.memset(b_f[:, :], 0.0))
            nc.gpsimd.memset(ones[:, :], 1.0).then_inc(ident_done, 1)
            pool.wait_ge(ident_done, 1)
            for i, f in enumerate(inv_freq()):
                last = nc.gpsimd.memset(freq_row[0:1, :].rearrange("a (q i) -> a q i", i=HD // 2)[:, :, i], float(f))
            done(last)
            done(nc.gpsimd.memset(sign[:, :], 1.0))
            done(nc.gpsimd.memset(sign[0:32, :], -1.0))
            done(nc.gpsimd.memset(sign[64:96, :], -1.0))
            done(nc.gpsimd.memset(mask_src, 0.0))
            done(nc.gpsimd.memset(mask_src[:, 0:P], NEG))
            for at, causal in ((1, 1), (2, 0), (3, 1), (4, 0), (5, 1)):
                m = mask_src[:, at * P:(at + 1) * P]
                sgn = 1 if causal else -1
                done(nc.gpsimd.affine_select(out=m, in_=m, compare_op=ALU.is_ge if causal else ALU.is_gt, fill=NEG,
                                             base=0, pattern=[[-sgn, P]], channel_multiplier=sgn))
            nc.gpsimd.memset(pool_flag[:, :], 0.0).then_inc(const_done, 1)
            pool.wait_ge(const_done, 1)

            pool.wait_ge(xt_ready, KT)
            pool.dma_start(rope[2].bitcast(I32), positions.broadcast_to([P, SEQ])).then_inc(pos_landed, 16)

            for p in range(2):
                for side in range(2):
                    _, q2, _, k2 = fox_ops(p, side)
                    o = HD * (1 - side)
                    done(nc.gpsimd.memset(q2[half(1 - side), :].bitcast(F32), 0.0))
                    done(nc.gpsimd.memset(k2[half(1 - side), :].bitcast(F32), 0.0))
                    done(nc.gpsimd.memset(q2[o:o + 4, :].bitcast(F32), -1.0))
                    done(nc.gpsimd.memset(k2[o:o + 4, :].bitcast(F32), 1.0))
            pool.wait_ge(c_done, 1)
            pool.dma_start(c_dram[:, 0, :], pt_hi[P - HEADS:P, 0:SEQ]).then_inc(c_stored, 16)
            pool.dma_start(c_dram[:, 1, :], pt_lo[P - HEADS:P, 0:SEQ]).then_inc(c_stored, 16)
            pool.wait_ge(c_stored, 32)
            for p in range(PAIRS):
                if p >= 2:
                    pool.wait_ge(s_ready, 2 * NB * (p - 1))
                for side in range(2):
                    _, q2, _, k2 = fox_ops(p, side)
                    o = HD * (1 - side)
                    landed = aug_landed[p % 2] if p else aug0_landed[side]
                    pool.dma_start(q2[o:o + 2, :], c_dram[2 * p + side]).then_inc(landed, 16)
                    pool.dma_start(k2[o + 2:o + 4, :], c_dram[2 * p + side]).then_inc(landed, 16)
                if p == 0:
                    continue
                pool.wait_ge(hi_done, 2 * p + 1)
                for side in range(2):
                    q1, q2, _, _ = fox_ops(p, side)
                    pool.dma_start(q2[half(side), :], q1[half(side), :]).then_inc(aug_landed[p % 2], 16)
                pool.wait_ge(hi_done, 2 * p + 2)
                for side in range(2):
                    k1 = fox_ops(p, side)[2]
                    pool.dma_start(k1[half(1 - side), :], k1[half(side), :]).then_inc(aug_landed[p % 2], 16)

            def add_squares(norm):
                for k in range(1, KT - 1):
                    pool.wait_ge(sq_done, norm * KT + k + 1)
                    n = (norm // 2 - 1) * (KT - 2) + k
                    if k >= 2:
                        pool.wait_ge(xsq_done, n - 1)
                    nc.gpsimd.tensor_tensor(sq_sum[:, :], sq_sum[:, :], tmp[:, k % 2, :], ALU.add).then_inc(xsq_done, 1)
                pool.wait_ge(xsq_done, norm // 2 * (KT - 2))

            add_squares(2)
            add_squares(4)

            pool.wait_ge(used, W_SWA)
            for kv in range(KV_HEADS):
                for side in range(2):
                    done(nc.gpsimd.memset(swa_k(kv, side)[1][half(1 - side), :].bitcast(F32), 0.0))
            nc.gpsimd.memset(pool_flag[:, :], 0.0).then_inc(aug_set, 1)

            def swap(i):
                pool.wait_ge(rot_done, i + 1)
                pool.wait_ge(rope_done, i - 1)
                for q in range(4):
                    pool.dma_start(swapped[i % 2][32 * (q ^ 1):32 * (q ^ 1) + 32, :],
                                   unrotated[i % 2][32 * q:32 * q + 32, :]).then_inc(swap_landed[i % 2], 16)

            def copy_q(p):
                pool.wait_ge(hi_done, 2 * PAIRS + 3 + p)
                for side in range(2):
                    q1, q2 = swa_q(p, side)
                    pool.dma_start(q1[half(side), :], q2[half(side), :]).then_inc(q_copied[p % 2], 16)
                pool.wait_ge(q_done, 2 + p)
                for side in range(2):
                    pool.dma_start(swa_q(p, side)[0][half(1 - side), :],
                                   swa_q_low(p)[half(side), :]).then_inc(q_copied[p % 2], 16)

            for p in range(DIRECT, PAIRS):
                swap(1 + p)
                copy_q(p)
            add_squares(6)

        @block.tensor
        def _(pe):
            def project(n, g, rhs_hi, rhs_lo, k0=0, k1=KT, first=True, last=True, rhs_ready=None, starts=True,
                        looped=False, rw=0, rg=0):
                if k0 == 0 and starts:
                    pe.wait_ge(wlo_done, n + 1 + rw)
                    if first and g >= 2:
                        pe.wait_ge(acc_free, groups_before(g, looped) + rg)
                s, a = n % RING, group_bank(g)
                for k in range(k0, k1):
                    if rhs_ready:
                        rhs_ready(k)
                    nc.tensor.matmul(a[:, :], w_hi[:, s, k, :], rhs_hi(k), start=first and k == 0, stop=False)
                    nc.tensor.matmul(a[:, :], w_hi[:, s, k, :], rhs_lo(k), start=False, stop=False)
                    mm = nc.tensor.matmul(a[:, :], w_lo[:, s, k, :], rhs_hi(k), start=False,
                                          stop=last and k == KT - 1)
                return mm

            def finish(mm):
                mm.then_inc(used, 1)

            def of(t):
                return lambda k: t[:, k, :]

            def stat(norm, k):
                pe.wait_ge(sq_done, norm * KT + k + 1)
                nc.tensor.matmul(mix[norm % 2][:, :], ones[:, :], tmp[:, k % 2, :], start=(k == 0),
                                 stop=(k == KT - 1)).then_inc(stat_done, 1)

            def post_stat(norm):
                pe.wait_ge(ssq_done, (norm // 2 + 1) * (KT - 2))
                nc.tensor.matmul(mix[norm % 2][:, :], ones[:, :], rstd[:, :], start=True,
                                 stop=False).then_inc(stat_done, 1)
                pe.wait_ge(sq_done, (norm + 1) * KT)
                nc.tensor.matmul(mix[norm % 2][:, :], ones[:, :], tmp[:, (KT - 1) % 2, :], start=False,
                                 stop=True).then_inc(stat_done, 1)

            pe.wait_ge(ident_done, 1)
            for b in range(NB):
                pe.wait_ge(x_landed[b], 16)
                for k in range(KT):
                    mm = nc.tensor.transpose(x_banks[k][:, b * P:(b + 1) * P], x_in[:, b, k * P:(k + 1) * P],
                                             ident[:, :])
                    if b == NB - 1:
                        mm.then_inc(xt_ready, 1)

            def x_stat(norm):
                pe.wait_ge(xsq_done, norm // 2 * (KT - 2))
                nc.tensor.matmul(mix[norm % 2][:, :], ones[:, :], sq_sum[:, :], start=True,
                                 stop=False).then_inc(stat_done, 1)
                pe.wait_ge(sq_done, (norm + 1) * KT)
                nc.tensor.matmul(mix[norm % 2][:, :], ones[:, :], tmp[:, (KT - 1) % 2, :], start=False,
                                 stop=True).then_inc(stat_done, 1)

            def first_tiles(n, g, norm, count):
                for k in range(KT):
                    if norm == 0:
                        stat(norm, k)
                    pe.wait_ge(h_done, norm // 2 * KT + k + 1)
                    for i in range(count):
                        if k == 0:
                            pe.wait_ge(wlo_done, n + i + 1)
                        mm = project(n + i, g + i, of(h_hi), of(h_lo), k, k + 1, starts=False)
                        if k == KT - 1:
                            finish(mm)
                if norm > 0:
                    x_stat(norm)

            pe.wait_ge(x_done, 3)
            first_tiles(W_FOX, G_FOX, 0, 1)
            pe.wait_ge(const_done, 1)
            nc.tensor.transpose(mix[1][:, 0:1], freq_row[0:1, :], ident[0:1, 0:1]).then_inc(freq_t, 1)


            def fox_proj(pair, k0, k1):
                if pair == PAIRS:
                    return
                while k0 < k1:
                    j, a = divmod(k0, KT)
                    b = min(KT, a + k1 - k0)
                    mm = project(W_FOX + 1 + 3 * pair + j, G_FOX + 1 + 3 * pair + j, of(h_hi), of(h_lo), a, b)
                    if b == KT:
                        finish(mm)
                    k0 += b - a

            def fox_logits(hd, qb):
                p, side = divmod(hd, 2)
                j = hd * NB + qb
                if side == 0 and qb == 0:
                    pe.wait_ge(qk_done, 2 * p + 2)
                    if p > 0:
                        pe.wait_ge(aug_landed[p % 2], 128 * ((p + 1) // 2))
                if p == 0 and qb == 0:
                    pe.wait_ge(aug0_landed[side], 32)
                if j == 0:
                    pe.wait_ge(mask_done, 1)
                if j >= 2:
                    pe.wait_ge(exp_done, j - 1)
                q1, q2, k1, k2 = fox_ops(p, side)
                n, qs = (qb + 1) * P, slice(qb * P, (qb + 1) * P)
                s = logit[j % 2]
                nc.tensor.matmul(s[:, 0:n], q1[:, qs], k1[:, 0:n], start=True, stop=False)
                nc.tensor.matmul(s[:, 0:n], q2[:, qs], k2[:, 0:n], start=False, stop=False)
                nc.tensor.matmul(s[:, qs], ident_r[:, :], masks[:, P:2 * P], start=False,
                                 stop=True).then_inc(s_ready, 1)

            def fox_transposes(hd, i):
                j = fox_t(hd, i)
                if i == 0:
                    pe.wait_ge(prob_done, hd + 1)
                if j >= 2:
                    pe.wait_ge(t_free, j - 1)
                at = 0
                for kb in ((0,), (1,), (2, 3))[i]:
                    for qb in range(kb, NB):
                        c = FOX_OFF[qb] + kb * P
                        mm = nc.tensor.transpose(trans[j % 2][:, at:at + P], prob[hd % 2][:, c:c + P], ident[:, :])
                        at += P
                mm.then_inc(t_ready, 1)

            def value_transposes(j, ready, count):
                pe.wait_ge(ready, count)
                if j >= 2:
                    pe.wait_ge(t_free, j - 1)
                for b in range(NB):
                    mm = nc.tensor.transpose(trans[j % 2][:, b * P:(b + 1) * P], tmp[:, 0, b * P:(b + 1) * P],
                                             ident[:, :])
                mm.then_inc(t_ready, 1)

            def fox_mix(hd):
                p = hd // 2
                pe.wait_ge(t_free, fox_t(hd, 2) + 1)
                if hd >= 2:
                    pe.wait_ge(o_done, hd - 1)
                o = mix[hd % 2]
                for kb in range(NB):
                    n = (NB - kb) * P
                    pt = slice(FOX_PT[kb], FOX_PT[kb] + n)
                    for v, t in ((v_hi, pt_hi), (v_hi, pt_lo), (v_lo, pt_hi)):
                        mm = nc.tensor.matmul(o[:, kb * P:SEQ], v[:, p % 2, kb, :], t[:, pt],
                                              start=(kb == 0 and v is v_hi and t is pt_hi),
                                              stop=(kb == NB - 1 and v is v_lo))
                mm.then_inc(pv_done, 1)

            def steps(at, n):
                end = min(at + n, 3 * KT * PAIRS)
                while at < end:
                    pair, k0 = divmod(at, 3 * KT)
                    k1 = min(3 * KT, k0 + end - at)
                    fox_proj(pair, k0, k1)
                    at += k1 - k0

            def early_out(w0, g0, heads0, k, o):
                pe.wait_ge(o_done, heads0 + 2 * k + 2)
                project(w0 + o, g0 + o, of(o_hi), of(o_lo), k, k + 1)

            steps(0, 3 * KT + 6)
            fox_logits(0, 0)
            fox_logits(0, 1)
            steps(3 * KT + 6, 2)
            fox_logits(0, 2)
            fox_logits(0, 3)
            for h in range(HEADS):
                nxt = h + 1 < HEADS
                at = 4 * KT + 12 * h
                out_steps = h >= HEADS - 2
                k_out = 3 * (h - HEADS + 2)

                def early(k):
                    if out_steps:
                        for o in range(2):
                            early_out(W_FOX_OUT, G_FOX_OUT, 0, k, o)

                steps(at, 2)
                if h % 2 == 0:
                    value_transposes(fox_t(h, 0) - 1, acc_free, G_FOX + 4 + 3 * (h // 2))
                if h >= 1:
                    fox_mix(h - 1)
                early_steps = 2 * (h % 2)
                steps(at + 2, early_steps)
                if nxt:
                    fox_logits(h + 1, 0)
                steps(at + 2 + early_steps, 3 - early_steps)
                early(k_out)
                fox_transposes(h, 0)
                if nxt:
                    fox_logits(h + 1, 1)
                steps(at + 5, 3)
                early(k_out + 1)
                fox_transposes(h, 1)
                if nxt:
                    fox_logits(h + 1, 2)
                steps(at + 8, 2)
                early(k_out + 2)
                fox_transposes(h, 2)
                if nxt:
                    fox_logits(h + 1, 3)
                steps(at + 10, 2)
            fox_mix(HEADS - 1)

            def out_proj(w0, g0, norm, heads0):
                for o in range(KT):
                    finish(project(w0 + o, g0 + o, of(o_hi), of(o_lo), EARLY if o < 2 else 0, KT, rhs_ready=(
                        lambda k: pe.wait_ge(o_done, heads0 + 2 * k + 2)) if o == 0 else None))
                post_stat(norm)

            def mlp(layer, norm):
                w0, g0 = W_MLP[layer], G_MLP[layer]
                first_tiles(w0, g0, norm, AHEAD)
                for i in range(AHEAD, RING):
                    finish(project(w0 + i, g0 + i, of(h_hi), of(h_lo)))
                for c in range(CHUNKS):
                    with pe.Fori(1 if c == 0 else 0, F_CHUNK // RING) as it:
                        r = it * RING
                        for i in range(RING):
                            finish(project(w0 + i, g0 + i, of(h_hi), of(h_lo), looped=True, rw=r, rg=r))
                    w0, g0 = w0 + F_CHUNK, g0 + F_CHUNK
                    done = (layer * CHUNKS + c) * F_CHUNK

                    def down(i, rw, rg):
                        for hf in range(HALVES):
                            def u(t):
                                return lambda k: t[:, hf * KT + k, :]

                            def u_ready(k):
                                pe.wait_ge(u_done, done + hf * KT + k + 1)
                            finish(project(w0 + i * HALVES + hf, g0 + i, u(u_hi), u(u_lo), first=hf == 0,
                                           last=hf == HALVES - 1, rhs_ready=u_ready if i == 0 else None,
                                           looped=True, rw=rw, rg=rg))
                    with pe.Fori(0, KT // RING) as it:
                        o = it * RING
                        for i in range(RING):
                            down(i, o * HALVES, o)
                    w0, g0 = w0 + KT * HALVES, g0 + KT
                post_stat(norm + 1)

            out_proj(W_FOX_OUT, G_FOX_OUT, 1, 0)
            mlp(0, 2)

            first_tiles(W_SWA, G_SWA, 4, 2)

            def swa_proj(pair, k0, k1):
                if pair >= PAIRS:
                    return
                mm = project(W_SWA + 2 + pair, G_SWA + 2 + pair, of(h_hi), of(h_lo), k0, k1)
                if k1 == KT:
                    finish(mm)

            def swa_logits(hd, i):
                p, side = divmod(hd, 2)
                j = FOX_S + hd * 2 + i
                if side == 0 and i == 0:
                    pe.wait_ge(q_done, p + 2)
                    if p >= DIRECT:
                        pe.wait_ge(q_copied[p % 2], 64 * (p // 2))
                    if p == 0:
                        pe.wait_ge(aug_set, 1)
                    if hd == GROUP:
                        pe.wait_ge(k_done, 1)
                pe.wait_ge(exp_done, j - 1)
                q1, q2 = swa_q(p, side)
                k1, k2 = swa_k(hd // GROUP, side)
                s = logit[j % 2]
                nc.tensor.matmul(s[:, :], ident_r[:, :], masks[:, 2 * i * P:(2 * i + 4) * P], start=True, stop=False)
                for e in range(2):
                    qb = 2 * i + e
                    k0 = max(qb - 1, 0) * P
                    to = s[:, e * 2 * P + (P if qb == 0 else 0):(e + 1) * 2 * P]
                    qs, ks = slice(qb * P, (qb + 1) * P), slice(k0, (qb + 1) * P)
                    nc.tensor.matmul(to, q1[:, qs], k1[:, ks], start=False, stop=False)
                    mm = nc.tensor.matmul(to, q2[:, qs], k2[:, ks], start=False, stop=e == 1)
                mm.then_inc(s_ready, 1)

            def swa_t(hd, i):
                return SWA_T0 + 2 * hd + i

            def swa_transposes(hd, i):
                j = swa_t(hd, i)
                if i == 0:
                    pe.wait_ge(prob_done, HEADS + hd + 1)
                    pe.wait_ge(scaled, hd + 1)
                pe.wait_ge(t_free, j - 1)
                for e in range(2):
                    kb = 2 * i + e
                    for own, qb in ((1, kb), (0, kb + 1)):
                        if qb < NB:
                            c = qb * 2 * P + own * P
                            at = e * 2 * P + (1 - own) * P
                            mm = nc.tensor.transpose(trans[j % 2][:, at:at + P], swa_prob[hd % 2][:, c:c + P], ident[:, :])
                mm.then_inc(t_ready, 1)

            def swa_mix(hd):
                pe.wait_ge(t_free, swa_t(hd, 1) + 1)
                pe.wait_ge(o_done, HEADS + hd - 1)
                o = mix[hd % 2]
                for kb in range(NB):
                    n = P * min(2, NB - kb)
                    for v, t in ((v_hi, pt_hi), (v_hi, pt_lo), (v_lo, pt_hi)):
                        mm = nc.tensor.matmul(o[:, kb * P:kb * P + n], v[:, 0, kb, :], t[:, kb * 2 * P:kb * 2 * P + n],
                                              start=(kb == 0 and v is v_hi and t is pt_hi), skip_group_check=True,
                                              stop=(kb == NB - 1 and v is v_lo))
                mm.then_inc(pv_done, 1)

            swa_proj(0, 0, KT)
            value_transposes(FOX_T, v_scaled, 1)
            swa_proj(1, 0, KT)
            swa_proj(2, 0, 4)
            swa_logits(0, 0)
            swa_logits(0, 1)
            swa_proj(2, 4, KT)
            for h in range(HEADS):
                pair, k0 = h // 2 + 3, h % 2 * 4
                nxt = h + 1 < HEADS
                out_steps = h >= HEADS - 2
                k_out = 3 * (h - HEADS + 2)

                def swa_early(k):
                    if out_steps:
                        for o in range(2):
                            early_out(W_SWA_OUT, G_SWA_OUT, HEADS, k, o)

                swa_proj(pair, k0, k0 + 1)
                if nxt:
                    swa_logits(h + 1, 0)
                swa_proj(pair, k0 + 1, k0 + 2)
                if nxt:
                    swa_logits(h + 1, 1)
                if h >= 1:
                    swa_mix(h - 1)
                swa_early(k_out)
                swa_transposes(h, 0)
                swa_proj(pair, k0 + 2, k0 + 3)
                swa_early(k_out + 1)
                swa_transposes(h, 1)
                swa_proj(pair, k0 + 3, k0 + 4)
                swa_early(k_out + 2)
            swa_mix(HEADS - 1)

            out_proj(W_SWA_OUT, G_SWA_OUT, 5, HEADS)
            mlp(1, 6)

            for k in range(KT):
                if k == KT - 1:
                    pe.wait_ge(rstd_done, 8)
                for b in range(NB):
                    nc.tensor.matmul(out_banks[k][:, b * P:(b + 1) * P], xT[:, k, b * P:(b + 1) * P], ident[:, :],
                                     start=b == 0, stop=False, skip_group_check=True)
            for k in range(KT):
                pe.wait_ge(yn_done, KT * 3 + k + 1)
                for b in range(NB):
                    mm = nc.tensor.matmul(out_banks[k][:, b * P:(b + 1) * P], yT[:, k, b * P:(b + 1) * P],
                                          ident[:, :], start=False, stop=True, skip_group_check=True)
                mm.then_inc(fin_ready, 1)

        @block.scalar
        def _(sc):
            def split(n, r=0):
                if n >= W_END:
                    return
                sc.wait_ge(raw_landed[n % RAW], 16 * (n // RAW + 1) + r * (16 // RAW))
                if n >= RING:
                    sc.wait_ge(used, n - RING + 1 + r)
                nc.scalar.activation(w_hi[:, n % RING, :, :], w_raw[:, n % RAW, :, :], ACT.Copy).then_inc(whi_done, 1)

            def squares(norm, k, src, ready, count):
                sc.wait_ge(ready, count)
                to = tmp[:, k % 2, :]
                if norm % 2:
                    if k == 0:
                        to = rstd[:, :]
                    elif k >= 3:
                        sc.wait_ge(ssq_done, norm // 2 * (KT - 2) + k - 2)
                elif norm == 0:
                    if k >= 2:
                        sc.wait_ge(stat_done, k - 1)
                elif k == 0:
                    to = sq_sum[:, :]
                elif k >= 3:
                    sc.wait_ge(xsq_done, (norm // 2 - 1) * (KT - 2) + k - 2)
                nc.scalar.activation(to, src, ACT.Square).then_inc(sq_done, 1)

            def root(norm):
                sc.wait_ge(stat_done, stats_before(norm + 1))
                if norm == 0:
                    sc.wait_ge(eps_set, 1)
                nc.scalar.activation(tmp[:, 3, :], mix[norm % 2][:, :], ACT.Ln, scale=1.0 / D,
                                     bias=eps[:, 0:1]).then_inc(r0_step, 1)
                sc.wait_ge(r0_step, 2 * norm + 1)
                nc.scalar.activation(tmp[:, 3, :], tmp[:, 3, :], ACT.Exp, scale=-0.5).then_inc(r0_step, 1)

            def pre_tiles(kind, layer, norm, n=0, ahead=0, splits=()):
                i = norm // 2
                for k in range(KT):
                    sc.wait_ge(x_done, i * KT + k + 1)
                    nc.scalar.activation(h_hi[:, k, :], xT[:, k, :], ACT.Copy,
                                         scale=gains[:, kind, layer, k:k + 1]).then_inc(hh_done, 1)
                    squares(norm, k, xT[:, k, :], x_done, i * KT + k + 1)
                    if k in splits:
                        split(1 + splits.index(k))
                for i in range(ahead):
                    split(n + i)
                root(norm)

            nc.scalar.preload_act_table_set("natural_log_exp_and_others")
            with nc.allow_non_contiguous_dma(reason="small vectors, feature-major"):
                for i, g in enumerate((norm_pre_mix, norm_post_mix, norm_pre_ffn, norm_post_ffn)):
                    for layer in range(2):
                        sc.dma_start(gains[:, i, layer, :], g[layer].rearrange("(k p) -> p k", p=P)).then_inc(
                            gain0_landed if i == layer == 0 else small_landed, 16)
                sc.wait_ge(ident_done, 1)
                sc.dma_start(b_f[P - HEADS:P, :], fox_b_f.rearrange("a h -> h a")).then_inc(small_landed, 16)
            sc.dma_start(sinks[:, :], swa_sinks.broadcast_to([P, HEADS])).then_inc(small_landed, 16)
            split(0)
            sc.wait_ge(const_done, 1)
            nc.scalar.activation(ident_r[:, :], ident[:, :], ACT.Copy)
            nc.scalar.activation(masks[:, :], mask_src, ACT.Copy).then_inc(mask_done, 1)
            sc.wait_ge(gain0_landed, 16)
            pre_tiles(0, 0, 0, W_FOX + AHEAD, 1, FIRST_SPLITS)

            gate_rows = slice(P - 32, P)
            sc.wait_ge(gate_step, 1)
            nc.scalar.activation(tmp[gate_rows, 3, :], tmp[gate_rows, 3, :], ACT.Exp).then_inc(gate_act, 1)
            sc.wait_ge(gate_step, 2)
            nc.scalar.activation(tmp[gate_rows, 0, :], tmp[gate_rows, 0, :], ACT.Ln).then_inc(gate_act, 1)

            def fox_exp(hd, qb):
                j, n = hd * NB + qb, (qb + 1) * P
                sc.wait_ge(max_done, j + 1)
                if hd >= 2 and qb == 0:
                    sc.wait_ge(t_ready, fox_t(hd - 2, 2) + 1)
                nc.scalar.activation(prob[hd % 2][:, FOX_OFF[qb]:FOX_OFF[qb] + n], logit[j % 2][:, 0:n], ACT.Exp,
                                     bias=nmax[:, hd % 2, qb:qb + 1],
                                     accum_out=rsum[:, hd % 2, qb:qb + 1]).then_inc(exp_done, 1)

            def fox_high_q(p):
                sc.wait_ge(acc_free, G_FOX + 2 + 3 * p)
                for side in range(2):
                    h = half(side)
                    for to in fox_ops(p, side)[0:2 if p == 0 else 1]:
                        last = nc.scalar.activation(to[h, :], fox_scaled(p)[0][h, :], ACT.Copy, scale=SCALE)
                last.then_inc(hi_done, 1)

            def fox_high_k(p):
                sc.wait_ge(acc_free, G_FOX + 3 + 3 * p)
                for side in range(2):
                    h = half(side)
                    for to in (side, 1 - side)[0:2 if p == 0 else 1]:
                        last = nc.scalar.activation(fox_ops(p, side)[2][half(to), :], fox_scaled(p)[1][h, :], ACT.Copy)
                last.then_inc(hi_done, 1)

            def high_v(j, slot):
                sc.wait_ge(t_ready, j + 1)
                nc.scalar.activation(v_hi[:, slot, :, :].rearrange("p b n -> p (b n)"), trans[j % 2][:, :],
                                     ACT.Copy).then_inc(vh_done, 1)

            def high_t(j, at, n, free):
                sc.wait_ge(t_ready, j + 1)
                if free:
                    sc.wait_ge(pv_done, free)
                nc.scalar.activation(pt_hi[:, at:at + n], trans[j % 2][:, 0:n], ACT.Copy).then_inc(th_done, 1)

            def fox_high_t(hd, i):
                high_t(fox_t(hd, i), FOX_PT[i], (512, 384, 384)[i], hd)

            def high_o(hd, rows):
                p, side = divmod(hd % HEADS, 2)
                sc.wait_ge(pv_done, hd + 1)
                nc.scalar.activation(o_hi[half(side), p, :], mix[hd % 2][rows, :], ACT.Copy).then_inc(oh_done, 1)

            fox_high_q(0)
            split(W_FOX + RING)
            split(W_FOX + 1 + RING)
            fox_high_k(0)
            split(W_FOX + 2 + RING)
            for qb in range(NB):
                fox_exp(0, qb)
            split(W_FOX + 3 + RING)
            for h in range(HEADS):
                even, p = h % 2 == 0, h // 2
                nxt, proj = h + 1 < HEADS, p + 1 < PAIRS
                t = W_FOX + 1 + 3 * (p + 1)
                if even:
                    high_v(7 * p, p % 2)
                if even and proj:
                    fox_high_q(p + 1)
                if h >= 1:
                    high_o(h - 1, half((h - 1) % 2))
                if nxt:
                    fox_exp(h + 1, 0)
                if not even and proj:
                    split(t + 1 + RING)
                fox_high_t(h, 0)
                if nxt:
                    fox_exp(h + 1, 1)
                if even and proj:
                    split(t + RING)
                if not even and p + 2 < PAIRS:
                    split(t + 2 + RING)
                fox_high_t(h, 1)
                if nxt:
                    fox_exp(h + 1, 2)
                if even and proj:
                    fox_high_k(p + 1)
                fox_high_t(h, 2)
                if nxt:
                    fox_exp(h + 1, 3)
                if h == TABLE_SLOT:
                    sc.wait_ge(angle_done, 1)
                    nc.scalar.activation(sin_t[:, :], rope[1], ACT.Sin, scale=sign[:, 0:1])
                    nc.scalar.activation(cos_t[:, :], rope[2], ACT.Sin).then_inc(table_done, 1)
                    nc.scalar.preload_act_table_set("natural_log_exp_and_others")
            high_o(HEADS - 1, half(1))

            def out_proj(layer, w0, g0, norm):
                for o in range(KT):
                    split(w0 + o + AHEAD)
                    squares(norm, o, yT[:, o, :], acc_free, g0 + o + 1)
                root(norm)
                pre_tiles(2, layer, norm + 1, w0 + KT + AHEAD, MLP_AHEAD)

            def mlp(layer, norm):
                n, g = W_MLP[layer], G_MLP[layer]
                for c in range(CHUNKS):
                    def hidden(j, r=0):
                        i = (layer * CHUNKS + c) * F_CHUNK + j
                        sc.wait_ge(acc_free, g + j + 1 + r)
                        nc.scalar.activation(u_hi[:, j + r, :], tmp[:, j % 2, :], ACT.Square).then_inc(uhi_done, 1)
                        if i >= 2:
                            sc.wait_ge(u_done, i - 1 + r)
                        nc.scalar.activation(tmp[:, 2 + j % 2, :], tmp[:, j % 2, :], ACT.Square).then_inc(squared, 1)

                    if c == 0:
                        for j in range(RING):
                            if j >= MLP_AHEAD:
                                split(n + j + AHEAD)
                            hidden(j)
                    with sc.Fori(1 if c == 0 else 0, F_CHUNK // RING) as it:
                        r = it * RING
                        for j in range(RING):
                            split(n + j + AHEAD, r)
                            hidden(j, r)
                    n, g = n + F_CHUNK, g + F_CHUNK
                    if c < CHUNKS - 1:
                        with sc.Fori(0, KT * HALVES // RING) as it:
                            r = it * RING
                            for i in range(RING):
                                split(n + i + AHEAD, r)
                    else:
                        for o in range(KT):
                            for hf in range(HALVES):
                                split(n + o * HALVES + hf + AHEAD)
                            squares(norm + 1, o, yT[:, o, :], acc_free, g + o + 1)
                    n, g = n + KT * HALVES, g + KT
                root(norm + 1)

            out_proj(0, W_FOX_OUT, G_FOX_OUT, 1)
            mlp(0, 2)
            pre_tiles(0, 1, 4)

            def swap_first(g, i):
                sc.wait_ge(used, g + 1 + W_SWA - G_SWA)
                if i == 1:
                    sc.wait_ge(rstd_done, 5)
                elif i == 2:
                    sc.wait_ge(rope_done, 1)
                for q in range(4):
                    last = nc.scalar.activation(swapped[i % 2][32 * (q ^ 1):32 * (q ^ 1) + 32, :],
                                                acc[g % 2][32 * q:32 * q + 32, :], ACT.Copy)
                last.then_inc(rot_done, 1)

            def unrotated_copy(g, i):
                sc.wait_ge(used, g + 1 + W_SWA - G_SWA)
                if i >= DIRECT + 3:
                    sc.wait_ge(swap_landed[i % 2], 64 * ((i - 3) // 2))
                nc.scalar.activation(unrotated[i % 2], acc[g % 2][:, :], ACT.Copy).then_inc(rot_done, 1)

            def swa_high_k(kv):
                sc.wait_ge(rope_done, 1)
                k1 = swa_k(kv, 0)[0]
                for to in range(2):
                    last = nc.scalar.activation(k1[half(to), :], k_rotated[half(kv), :], ACT.Copy)
                last.then_inc(hi_done, 1)

            def swa_high_q(p):
                sc.wait_ge(rope_done, 2 + p)
                if p < DIRECT:
                    for side in range(2):
                        nc.scalar.activation(swa_q(p, side)[0][half(side), :], rope[2][half(side), :], ACT.Copy,
                                             scale=SCALE)
                nc.scalar.activation(swa_q(p, 0)[1], rope[2], ACT.Copy, scale=SCALE).then_inc(hi_done, 1)

            def swa_scale(hd):
                sc.wait_ge(rden_done, hd + 1)
                for qb in range(DVE_SCALES, NB):
                    pr = swa_prob[hd % 2][:, qb * 2 * P:(qb + 1) * 2 * P]
                    last = nc.scalar.activation(pr, pr, ACT.Copy, scale=rden[:, hd % 2, qb:qb + 1])
                last.then_inc(scaled, 1)

            def swa_exp(hd, i):
                j = FOX_S + hd * 2 + i
                sc.wait_ge(max_done, j + 1)
                if i == 0:
                    if hd >= 2:
                        sc.wait_ge(t_ready, SWA_T0 + 2 * (hd - 2) + 2)
                for e in range(2):
                    qb = 2 * i + e
                    last = nc.scalar.activation(swa_prob[hd % 2][:, qb * 2 * P:(qb + 1) * 2 * P],
                                                logit[j % 2][:, e * 2 * P:(e + 1) * 2 * P], ACT.Exp,
                                                bias=nmax[:, hd % 2, qb:qb + 1],
                                                accum_out=rsum[:, hd % 2, qb:qb + 1])
                last.then_inc(exp_done, 1)
                if i == 1:
                    nc.scalar.activation(esink[:, hd % 2, :], nmax[:, hd % 2, :], ACT.Exp,
                                         bias=sinks[:, hd:hd + 1]).then_inc(es_done, 1)

            def swa_high_t(hd, i):
                high_t(SWA_T0 + 2 * hd + i, i * 512, (512, 384)[i], HEADS + hd)

            swap_first(G_SWA + 1, 0)
            split(W_SWA + AHEAD)
            swap_first(G_SWA + 2, 1)
            swa_high_k(0)
            split(W_SWA + RING)
            high_v(FOX_T, 0)
            swa_high_q(0)
            swap_first(G_SWA + 3, 2)
            split(W_SWA + 1 + RING)
            swa_exp(0, 0)
            swa_high_q(1)
            swa_exp(0, 1)
            split(W_SWA + 2 + RING)
            split(W_SWA + 3 + RING)
            swa_scale(0)
            for h in range(HEADS):
                even, p = h % 2 == 0, h // 2
                nxt, rotates = h + 1 < HEADS, p + 2 < PAIRS
                if even and rotates:
                    unrotated_copy(G_SWA + 2 + p + 2, 3 + p)
                if nxt:
                    swa_exp(h + 1, 0)
                if not even and p + 3 < PAIRS:
                    split(W_SWA + 4 + p + RING)
                if h >= 1:
                    high_o(HEADS + h - 1, half((h - 1) // GROUP))
                if not even and rotates:
                    swa_high_q(p + 2)
                swa_high_t(h, 0)
                if nxt:
                    swa_exp(h + 1, 1)
                swa_high_t(h, 1)
                if nxt:
                    swa_scale(h + 1)
                if h == 0:
                    swa_high_k(1)
            high_o(2 * HEADS - 1, half(1))

            out_proj(1, W_SWA_OUT, G_SWA_OUT, 5)
            mlp(1, 6)
            for k in range(KT):
                sc.wait_ge(fin_ready, k + 1)
                nc.scalar.activation(yT[:, k, :], out_banks[k][:, :], ACT.Copy).then_inc(fin_done, 1)

        @block.vector
        def _(ve):
            steps = [0]

            def own(ins):
                steps[0] += 1
                ins.then_inc(dve_step, 1)
                ve.wait_ge(dve_step, steps[0])

            f32 = lambda ap: ap.bitcast(F32)

            def split(n, r=0):
                if n >= W_END:
                    return
                ve.wait_ge(whi_done, n + 1 + r)
                nc.vector.tensor_tensor(w_lo[:, n % RING, :, :], w_raw[:, n % RAW, :, :],
                                        f32(w_hi[:, n % RING, :, :]), ALU.subtract).then_inc(wlo_done, 1)

            def root(norm, n=None):
                ve.wait_ge(r0_step, 2 * norm + 1)
                own(nc.vector.tensor_scalar(tmp[:, 2, :], mix[norm % 2][:, :], -0.5 / D, -0.5 * EPS, ALU.mult, ALU.add))
                if n is not None:
                    split(n)
                ve.wait_ge(r0_step, 2 * norm + 2)
                own(nc.vector.tensor_tensor(tmp[:, 2, :], tmp[:, 2, :], tmp[:, 3, :], ALU.mult))
                own(nc.vector.tensor_tensor(tmp[:, 2, :], tmp[:, 2, :], tmp[:, 3, :], ALU.mult))
                nc.vector.scalar_tensor_tensor(rstd[:, :], tmp[:, 2, :], 1.5, tmp[:, 3, :], ALU.add,
                                               ALU.mult).then_inc(rstd_done, 1)
                ve.wait_ge(rstd_done, norm + 1)

            def add_squares(norm, k):
                if 1 <= k <= KT - 2:
                    if k >= 2:
                        ve.wait_ge(ssq_done, norm // 2 * (KT - 2) + k - 1)
                    ve.wait_ge(sq_done, norm * KT + k + 1)
                    nc.vector.tensor_tensor(rstd[:, :], rstd[:, :], tmp[:, k % 2, :], ALU.add).then_inc(ssq_done, 1)

            def scaled_y(kind, layer, k, before):
                if k >= 2:
                    ve.wait_ge(x_done, before + k - 1)
                nc.vector.scalar_tensor_tensor(tmp[:, 2 + k % 2, :], yT[:, k, :], gains[:, kind, layer, k:k + 1],
                                               rstd[:, :], ALU.mult, ALU.mult).then_inc(yn_done, 1)

            def add_y(k, count):
                ve.wait_ge(yn_done, count)
                nc.vector.tensor_tensor(xT[:, k, :], xT[:, k, :], tmp[:, 2 + k % 2, :], ALU.add).then_inc(x_done, 1)

            def low_h(kind, layer, k, base):
                ve.wait_ge(hh_done, base + k + 1)
                nc.vector.scalar_tensor_tensor(h_lo[:, k, :], xT[:, k, :], gains[:, kind, layer, k:k + 1],
                                               f32(h_hi[:, k, :]), ALU.mult, ALU.subtract).then_inc(h_done, 1)

            def post_pre(kind, layer, norm, kind2, layer2):
                root(norm)
                base, before = (norm + 1) // 2 * KT, norm // 2 * KT

                scaled_y(kind, layer, 0, base)
                for k in range(KT):
                    if k + 1 < KT:
                        scaled_y(kind, layer, k + 1, base)
                    add_y(k, before + k + 1)
                    if k >= 1:
                        low_h(kind2, layer2, k - 1, base)
                low_h(kind2, layer2, KT - 1, base)
            def gates():
                r = slice(P - 32, P)
                z, e, u, c = (tmp[r, i, :] for i in (1, 3, 0, 2))
                ve.wait_ge(used, W_FOX + 1)
                nc.vector.tensor_tensor(z, acc[G_FOX % 2][r, :], rstd[r, :], ALU.mult).then_inc(acc_free, 1)
                ve.wait_ge(acc_free, G_FOX + 1)
                own(nc.vector.tensor_scalar(z, z, b_f[r, 0:1], None, ALU.add))
                nc.vector.scalar_tensor_tensor(e, z, -1.0, z, ALU.mult, ALU.min).then_inc(gate_step, 1)
                fox_scale(0, 0)
                ve.wait_ge(gate_act, 1)
                own(nc.vector.tensor_scalar(u, e, 1.0, None, ALU.add))
                own(nc.vector.scalar_tensor_tensor(e, u, -1.0, e, ALU.add, ALU.subtract))
                nc.vector.memset(c, 0.0).then_inc(gate_step, 1)
                ve.wait_ge(gate_act, 2)
                own(nc.vector.tensor_tensor(u, u, e, ALU.subtract))
                own(nc.vector.scalar_tensor_tensor(z, z, 0.0, u, ALU.min, ALU.subtract))
                own(nc.vector.tensor_tensor_scan(e, z, c, 0.0, ALU.add, ALU.add))
                own(nc.vector.tensor_copy(pt_hi[r, 0:SEQ], e))
                nc.vector.tensor_tensor(pt_lo[r, 0:SEQ], e, f32(pt_hi[r, 0:SEQ]), ALU.subtract).then_inc(c_done, 1)

            def low_q(src, q1, high, end):
                for side in range(2):
                    last = nc.vector.scalar_tensor_tensor(q1[side][half(1 - side), :], src[half(side), :], SCALE,
                                                          f32(high[side][half(side), :]), ALU.mult, ALU.subtract)
                last.then_inc(end, 1)

            def fox_scale(p, i):
                ve.wait_ge(used, W_FOX + 2 + 3 * p + i)
                if p >= 2:
                    ve.wait_ge(qk_done, 2 * p - 1 + i)
                nc.vector.tensor_tensor(fox_scaled(p)[i], acc[(G_FOX + 1 + 3 * p + i) % 2][:, :], rstd[:, :],
                                        ALU.mult).then_inc(acc_free, 1)

            def fox_low_q(p):
                ve.wait_ge(hi_done, 2 * p + 1)
                q1 = [fox_ops(p, s)[0] for s in range(2)]
                low_q(fox_scaled(p)[0], q1, q1, qk_done)

            def fox_low_k(p):
                ve.wait_ge(hi_done, 2 * p + 2)
                for side in range(2):
                    _, _, k1, k2 = fox_ops(p, side)
                    h = half(side)
                    last = nc.vector.tensor_tensor(k2[h, :], fox_scaled(p)[1][h, :], f32(k1[h, :]), ALU.subtract)
                last.then_inc(qk_done, 1)

            def fox_value(p):
                ve.wait_ge(used, W_FOX + 4 + 3 * p)
                nc.vector.tensor_tensor(tmp[:, 0, :], acc[(G_FOX + 3 + 3 * p) % 2][:, :], rstd[:, :],
                                        ALU.mult).then_inc(acc_free, 1)

            def swa_value_copy(n, g):
                ve.wait_ge(used, n + 1)
                nc.vector.tensor_copy(tmp[:, 0, :], acc[g % 2][:, :]).then_inc(acc_free, 1)

            def low_v(j, slot, i):
                ve.wait_ge(vh_done, i + 1)
                nc.vector.tensor_tensor(v_lo[:, slot, :, :].rearrange("p b n -> p (b n)"), trans[j % 2][:, :],
                                        f32(v_hi[:, slot, :, :].rearrange("p b n -> p (b n)")),
                                        ALU.subtract).then_inc(t_free, 1)

            def low_t(i, j, at, n):
                ve.wait_ge(th_done, i + 1)
                nc.vector.tensor_tensor(pt_lo[:, at:at + n], trans[j % 2][:, 0:n], f32(pt_hi[:, at:at + n]),
                                        ALU.subtract).then_inc(t_free, 1)

            def fox_low_t(hd, i):
                low_t(3 * hd + i, fox_t(hd, i), FOX_PT[i], (512, 384, 384)[i])

            def swa_low_t(hd, i):
                low_t(3 * HEADS + 2 * hd + i, SWA_T0 + 2 * hd + i, i * 512, (512, 384)[i])

            def low_o(hd, rows):
                p, side = divmod(hd % HEADS, 2)
                ve.wait_ge(oh_done, hd + 1)
                nc.vector.tensor_tensor(o_lo[half(side), p, :], mix[hd % 2][rows, :], f32(o_hi[half(side), p, :]),
                                        ALU.subtract).then_inc(o_done, 1)

            def fox_max(hd, qb):
                j = hd * NB + qb
                ve.wait_ge(s_ready, j + 1)
                nc.vector.reduce_max(nmax[:, hd % 2, qb:qb + 1], logit[j % 2][:, 0:(qb + 1) * P], AX_X,
                                     negate=True).then_inc(max_done, 1)

            def fox_norm(hd):
                ve.wait_ge(exp_done, (hd + 1) * NB)
                own(nc.vector.reciprocal(rden[:, hd % 2, :], rsum[:, hd % 2, :]))
                for qb in range(NB):
                    pr = prob[hd % 2][:, FOX_OFF[qb]:FOX_OFF[qb] + (qb + 1) * P]
                    last = nc.vector.tensor_scalar(pr, pr, rden[:, hd % 2, qb:qb + 1], None, ALU.mult)
                last.then_inc(prob_done, 1)

            def swa_max(hd, i):
                j = FOX_S + hd * 2 + i
                ve.wait_ge(s_ready, j + 1)
                nm = nmax[:, hd % 2, 2 * i:2 * i + 2]
                own(nc.vector.reduce_max(nm, logit[j % 2][:, :].rearrange("p (e n) -> p e n", e=2), AX_X, negate=True))
                nc.vector.tensor_scalar(nm, nm, nsinks[:, hd:hd + 1], None, ALU.min).then_inc(max_done, 1)

            def swa_norm(hd):
                ve.wait_ge(es_done, hd + 1)
                own(nc.vector.tensor_tensor(rden[:, hd % 2, :], rsum[:, hd % 2, :], esink[:, hd % 2, :], ALU.add))
                nc.vector.reciprocal(rden[:, hd % 2, :], rden[:, hd % 2, :]).then_inc(rden_done, 1)
                ve.wait_ge(rden_done, hd + 1)
                for qb in range(DVE_SCALES):
                    pr = swa_prob[hd % 2][:, qb * 2 * P:(qb + 1) * 2 * P]
                    last = nc.vector.tensor_scalar(pr, pr, rden[:, hd % 2, qb:qb + 1], None, ALU.mult)
                last.then_inc(prob_done, 1)

            def rotate_cos(g, i):
                ve.wait_ge(rot_done, i + 1)
                if i >= 1:
                    ve.wait_ge(rope_done, i)
                nc.vector.tensor_tensor(rope[1], acc[g % 2][:, :], cos_t[:, :], ALU.mult).then_inc(acc_free, 1)

            def rotate_sin(i):
                if i > DIRECT:
                    ve.wait_ge(swap_landed[i % 2], 64 * ((i - 1) // 2))
                own(nc.vector.tensor_tensor(swapped[i % 2], swapped[i % 2], sin_t[:, :], ALU.mult))
                if i >= 2:
                    ve.wait_ge(q_done, i)
                nc.vector.tensor_tensor(k_rotated if i == 0 else rope[2], swapped[i % 2], rope[1],
                                        ALU.add).then_inc(rope_done, 1)

            def swa_low_k(kv, hi, end):
                ve.wait_ge(hi_done, hi)
                for side in range(2):
                    k1, k2 = swa_k(kv, side)
                    last = nc.vector.tensor_tensor(k2[half(side), :], k_rotated[half(kv), :], f32(k1[half(kv), :]),
                                                   ALU.subtract)
                last.then_inc(end, 1)

            def swa_low_q(p):
                if p < DIRECT:
                    ve.wait_ge(hi_done, 2 * PAIRS + 2 + p)
                    low_q(rope[2], [swa_q(p, s)[0] for s in range(2)], [swa_q(p, s)[1] for s in range(2)], q_done)
                else:
                    ve.wait_ge(hi_done, 2 * PAIRS + 3 + p)
                    nc.vector.scalar_tensor_tensor(swa_q_low(p), rope[2], SCALE, f32(swa_q(p, 0)[1]), ALU.mult,
                                                   ALU.subtract).then_inc(q_done, 1)

            def out_proj(w0, g0, norm):
                for o in range(KT):
                    split(w0 + o + AHEAD)
                    ve.wait_ge(used, w0 + o + 1)
                    nc.vector.tensor_copy(yT[:, o, :], acc[(g0 + o) % 2][:, :]).then_inc(acc_free, 1)
                    add_squares(norm, o - 1)

            def mlp(layer, norm):
                n, g = W_MLP[layer], G_MLP[layer]
                for c in range(CHUNKS):
                    def hidden(j, r=0):
                        i = (layer * CHUNKS + c) * F_CHUNK + j
                        ve.wait_ge(used, n + j + 1 + r)
                        if i >= 2:
                            ve.wait_ge(squared, i - 1 + r)
                        nc.vector.scalar_tensor_tensor(tmp[:, j % 2, :], group_bank(g + j)[:, :], 0.0, rstd[:, :],
                                                       ALU.max, ALU.mult).then_inc(acc_free, 1)
                        ve.wait_ge(squared, i + 1 + r)
                        nc.vector.tensor_tensor(u_lo[:, j + r, :], tmp[:, 2 + j % 2, :], f32(u_hi[:, j + r, :]),
                                                ALU.subtract).then_inc(u_done, 1)

                    if c == 0:
                        for j in range(RING):
                            if j >= MLP_AHEAD:
                                split(n + j + AHEAD)
                            hidden(j)
                    with ve.Fori(1 if c == 0 else 0, F_CHUNK // RING) as it:
                        r = it * RING
                        for j in range(RING):
                            split(n + j + AHEAD, r)
                            hidden(j, r)
                    n, g = n + F_CHUNK, g + F_CHUNK
                    if c < CHUNKS - 1:
                        with ve.Fori(0, KT // RING) as it:
                            r = it * RING
                            for o in range(RING):
                                for hf in range(HALVES):
                                    split(n + o * HALVES + hf + AHEAD, r * HALVES)
                                ve.wait_ge(used, n + (o + 1) * HALVES + r * HALVES)
                                nc.vector.tensor_copy(yT[:, o + r, :], group_bank(g + o)[:, :]).then_inc(acc_free, 1)
                    else:
                        for o in range(KT):
                            for hf in range(HALVES):
                                split(n + o * HALVES + hf + AHEAD)
                            ve.wait_ge(used, n + (o + 1) * HALVES)
                            nc.vector.tensor_tensor(yT[:, o, :], group_bank(g + o)[:, :], yT[:, o, :],
                                                    ALU.add).then_inc(acc_free, 1)
                            add_squares(norm, o - 1)
                    n, g = n + KT * HALVES, g + KT

            def angles(part):
                turns, ang, quarter = rope[0], rope[1], rope[2]
                pieces = two_pi_parts()
                pi = 3.1415925
                if part == 0:
                    ve.wait_ge(pos_landed, 16)
                    ve.wait_ge(freq_t, 1)
                    own(nc.vector.tensor_copy(turns, rope[2].bitcast(I32)))
                    own(nc.vector.tensor_copy(freq[:, :], mix[1][:, 0:1]))
                elif part == 1:
                    own(nc.vector.tensor_scalar(ang, turns, freq[:, 0:1], None, ALU.mult))
                    magic = 1.5 * 2.0 ** 23
                    own(nc.vector.tensor_scalar(turns, ang, 0.5 / np.pi, magic, ALU.mult, ALU.add))
                    own(nc.vector.tensor_scalar(turns, turns, -magic, None, ALU.add))
                elif part < 5:
                    for piece in pieces[2 * (part - 2):2 * (part - 1)]:
                        own(nc.vector.scalar_tensor_tensor(ang, turns, -piece, ang, ALU.mult, ALU.add))
                elif part == 5:
                    own(nc.vector.tensor_scalar(ang, ang, pi, -pi, ALU.min, ALU.max))
                    own(nc.vector.tensor_scalar(quarter, ang, np.pi / 2, None, ALU.add))
                elif part == 6:
                    own(nc.vector.tensor_scalar(turns, quarter, pi, -2 * np.pi, ALU.is_gt, ALU.mult))
                    own(nc.vector.tensor_tensor(quarter, quarter, turns, ALU.add))
                    nc.vector.tensor_scalar(quarter, quarter, pi, -pi, ALU.min, ALU.max).then_inc(angle_done, 1)

            nc.vector.memset(eps[:, :], EPS).then_inc(eps_set, 1)
            split(0)
            for k in range(KT):
                ve.wait_ge(xt_ready, k + 1)
                if k == 0:
                    ve.wait_ge(mask_done, 1)
                nc.vector.tensor_copy(xT[:, k, :], x_banks[k][:, :]).then_inc(x_done, 1)
                if k == 0:
                    ve.wait_ge(gain0_landed, 16)
                if k - 1 in FIRST_SPLITS:
                    split(1 + FIRST_SPLITS.index(k - 1))
                if k >= 1:
                    low_h(0, 0, k - 1, 0)
            low_h(0, 0, KT - 1, 0)
            ve.wait_ge(small_landed, 16 * 9)
            own(nc.vector.tensor_scalar(nsinks[:, :], sinks[:, :], -1.0, None, ALU.mult))
            root(0, W_FOX + AHEAD)

            gates()
            split(W_FOX + RING)
            fox_low_q(0)
            fox_scale(0, 1)
            split(W_FOX + 1 + RING)
            fox_low_k(0)
            fox_value(0)
            split(W_FOX + 2 + RING)
            angles(0)
            for qb in range(NB):
                fox_max(0, qb)
            split(W_FOX + 3 + RING)
            fox_norm(0)
            for h in range(HEADS):
                even, p = h % 2 == 0, h // 2
                nxt, proj = h + 1 < HEADS, p + 1 < PAIRS
                t = W_FOX + 1 + 3 * (p + 1)
                if even and proj:
                    fox_scale(p + 1, 0)
                if even:
                    low_v(7 * p, p % 2, p)
                if nxt:
                    fox_max(h + 1, 0)
                if even and proj:
                    fox_low_q(p + 1)
                if h >= 1:
                    low_o(h - 1, half((h - 1) % 2))
                if not even and proj:
                    fox_value(p + 1)
                    split(t + 1 + RING)
                if nxt:
                    fox_max(h + 1, 1)
                fox_low_t(h, 0)
                if even and proj:
                    split(t + RING)
                if not even and p + 2 < PAIRS:
                    split(t + 2 + RING)
                if even and proj:
                    fox_scale(p + 1, 1)
                if nxt:
                    fox_max(h + 1, 2)
                fox_low_t(h, 1)
                if nxt:
                    fox_max(h + 1, 3)
                fox_low_t(h, 2)
                if even and proj:
                    fox_low_k(p + 1)
                if nxt:
                    fox_norm(h + 1)
                if not even:
                    angles(p + 1)
            low_o(HEADS - 1, half(1))

            out_proj(W_FOX_OUT, G_FOX_OUT, 1)
            post_pre(1, 0, 1, 2, 0)
            for i in range(MLP_AHEAD):
                split(W_MLP[0] + AHEAD + i)
            root(2)
            mlp(0, 3)
            post_pre(3, 0, 3, 0, 1)

            ve.wait_ge(stat_done, stats_before(5))
            swa_value_copy(W_SWA, G_SWA)
            root(4)
            ve.wait_ge(table_done, 1)
            own(nc.vector.tensor_tensor(cos_t[:, :], cos_t[:, :], rstd[:, :], ALU.mult))
            rotate_cos(G_SWA + 1, 0)
            nc.vector.tensor_tensor(tmp[:, 0, :], tmp[:, 0, :], rstd[:, :], ALU.mult).then_inc(v_scaled, 1)
            split(W_SWA + AHEAD)
            own(nc.vector.tensor_tensor(sin_t[:, :], sin_t[:, :], rstd[:, :], ALU.mult))
            rotate_sin(0)
            rotate_cos(G_SWA + 2, 1)
            swa_low_k(0, 2 * PAIRS + 1, q_done)
            rotate_sin(1)
            split(W_SWA + RING)
            low_v(FOX_T, 0, PAIRS)
            swa_low_q(0)
            rotate_cos(G_SWA + 3, 2)
            split(W_SWA + 1 + RING)
            rotate_sin(2)
            swa_max(0, 0)
            swa_max(0, 1)
            swa_low_q(1)
            split(W_SWA + 2 + RING)
            swa_norm(0)
            split(W_SWA + 3 + RING)
            for h in range(HEADS):
                even, p = h % 2 == 0, h // 2
                nxt, rotates = h + 1 < HEADS, p + 2 < PAIRS
                if nxt:
                    swa_max(h + 1, 0)
                if even and rotates:
                    rotate_cos(G_SWA + 2 + p + 2, 3 + p)
                if not even and rotates:
                    rotate_sin(3 + p)
                if nxt:
                    swa_max(h + 1, 1)
                if h >= 1:
                    low_o(HEADS + h - 1, half((h - 1) // GROUP))
                if not even and rotates:
                    swa_low_q(p + 2)
                swa_low_t(h, 0)
                swa_low_t(h, 1)
                if nxt:
                    swa_norm(h + 1)
                if h == 0:
                    swa_low_k(1, 2 * PAIRS + 4, k_done)
                if not even and p + 3 < PAIRS:
                    split(W_SWA + 4 + p + RING)
            low_o(2 * HEADS - 1, half(1))

            out_proj(W_SWA_OUT, G_SWA_OUT, 5)
            post_pre(1, 1, 5, 2, 1)
            for i in range(MLP_AHEAD):
                split(W_MLP[1] + AHEAD + i)
            root(6)
            mlp(1, 7)
            root(7)
            for k in range(KT):
                nc.vector.scalar_tensor_tensor(yT[:, k, :], yT[:, k, :], gains[:, 3, 1, k:k + 1], rstd[:, :],
                                               ALU.mult, ALU.mult).then_inc(yn_done, 1)


_INS = ["x", "positions", "fox_w_in", "fox_b_f", "fox_w_out", "swa_w_in", "swa_sinks", "swa_w_out",
        "norm_pre_mix", "norm_post_mix", "norm_pre_ffn", "norm_post_ffn", "mlp_w_up", "mlp_w_down"]


def kernel(**inputs):
    import numpy as _np
    import concourse.bacc as _bacc
    from concourse import mybir as _mybir
    from concourse.bass_utils import run_bass_kernel_spmd as _run

    nc = _bacc.Bacc("TRN2", target_bir_lowering=False, num_devices=1)
    arrays, args = {}, []
    for name in _INS:
        a = _np.ascontiguousarray(inputs[name])
        arrays[f"in_{name}_dram"] = a
        args.append(nc.dram_tensor(f"in_{name}_dram", a.shape, _mybir.dt.from_np(a.dtype), kind="ExternalInput").ap())
    args.append(nc.dram_tensor("out_0_dram", (1, SEQ, D), F32, kind="ExternalOutput").ap())
    trunk(nc, *args)
    r = _run(nc, [arrays], core_ids=[0])
    return r.results[0]["out_0_dram"]
```
